# Optimizing a Trainium2 kernel written in Bass

```python
import jax, jax.numpy as jnp
from jax import lax
import numpy as np

D_MODEL = 1024
BATCH = 1
SEQ = 1024
DEPTH = 2

HEAD_DIM = 32
SB_HEADS = 4
NSA_HEADS = 4
MOBA_HEADS = 4
Q_BLOCK = 128
SB_KTILE = 64
NSA_CMP_LEN = 32
NSA_CMP_STRIDE = 16
NSA_SEL_LEN = 64
NSA_TOP_N = 8
NSA_WINDOW = 512
MOBA_BLOCK = 256
MOBA_TOPK = 3
PEER_HEADS = 4
PEER_NKEYS = 128
PEER_N_EXPERTS = PEER_NKEYS * PEER_NKEYS
PEER_TOPK = 8
PEER_QDIM = 256
TOK_BLOCK = 128

N_BRANCHES = 3
SB_W = SB_HEADS * HEAD_DIM
NSA_W = NSA_HEADS * HEAD_DIM
MOBA_W = MOBA_HEADS * HEAD_DIM
IN_WIDTHS = (SB_W, SB_W, SB_W, NSA_W, HEAD_DIM, HEAD_DIM, HEAD_DIM, HEAD_DIM, HEAD_DIM, HEAD_DIM, 3 * NSA_HEADS, MOBA_W, HEAD_DIM, HEAD_DIM, N_BRANCHES * D_MODEL)
IN_WIDTH = sum(IN_WIDTHS)
DEEPNORM_ALPHA = (2.0 * DEPTH) ** 0.25
DEEPNORM_BETA = (8.0 * DEPTH) ** -0.25
LN_EPS = 1e-5

kernel_name = 'hybrid_sb_nsa_moba_peer_deepnorm'

def layer_norm(x, g, b):
    xf = x.astype(jnp.float32)
    mu = jnp.mean(xf, axis=-1, keepdims=True)
    var = jnp.mean(jnp.square(xf - mu), axis=-1, keepdims=True)
    return ((xf - mu) * lax.rsqrt(var + LN_EPS) * g + b).astype(x.dtype)

def masked_softmax(z, mask):
    z = jnp.where(mask, z.astype(jnp.float32), -jnp.inf)
    m = jnp.max(z, axis=-1, keepdims=True)
    m = jnp.where(jnp.isfinite(m), m, 0.0)
    p = jnp.exp(z - m)
    return p / jnp.maximum(jnp.sum(p, axis=-1, keepdims=True), 1e-30)

def alibi_slopes(n):
    return jnp.asarray([2.0 ** (-8.0 * (i + 1) / n) for i in range(n)], jnp.float32)

def stick_breaking_attention(q, k, v):
    B, H, S, dh = q.shape
    q = q * (dh ** -0.5)
    nkt = S // SB_KTILE
    kt = k.reshape(B, H, nkt, SB_KTILE, dh)
    vt = v.reshape(B, H, nkt, SB_KTILE, dh)
    tri = jnp.asarray(np.tril(np.ones((SB_KTILE, SB_KTILE), np.float32), k=-1))
    outs = []
    for i in range(S // Q_BLOCK):
        q0 = i * Q_BLOCK
        n = (q0 + Q_BLOCK) // SB_KTILE
        qb = q[:, :, q0:q0 + Q_BLOCK]
        z = jnp.einsum('bhqd,bhnkd->bhqnk', qb, kt[:, :, :n]).astype(jnp.float32)
        kpos = jnp.arange(n * SB_KTILE).reshape(n, SB_KTILE)
        qpos = q0 + jnp.arange(Q_BLOCK)
        past = kpos[None] < qpos[:, None, None]
        ls = jnp.where(past, -jax.nn.softplus(z), 0.0)
        tot = jnp.sum(ls, axis=-1)
        carry = lax.cumsum(tot, axis=3, reverse=True) - tot
        excl = jnp.einsum('bhqnj,js->bhqns', ls, tri) + carry[..., None]
        w = jnp.where(past, jnp.exp(z + ls + excl), 0.0)
        outs.append(jnp.einsum('bhqnk,bhnkd->bqhd', w.astype(v.dtype), vt[:, :, :n]))
    return jnp.concatenate(outs, axis=1).reshape(B, S, H * dh)

def nsa_attention(q, k_cmp, v_cmp, k_slc, v_slc, k_win, v_win, gates, pe_k, pe_v, w_ck, w_cv, slopes):
    B, S, H, dh = q.shape
    scale = dh ** -0.5
    nchunk = S // NSA_CMP_STRIDE
    nc = nchunk - 1

    def compress(t, pe, w):
        c = t.reshape(B, nchunk, NSA_CMP_STRIDE, dh)
        blocks = jnp.concatenate([c[:, :-1], c[:, 1:]], axis=2) + pe
        return jnp.einsum('bnf,fd->bnd', blocks.reshape(B, nc, NSA_CMP_LEN * dh), w)

    kc = compress(k_cmp, pe_k, w_ck)
    vc = compress(v_cmp, pe_v, w_cv)
    cend = jnp.arange(nc) * NSA_CMP_STRIDE + (NSA_CMP_LEN - 1)
    nsel = S // NSA_SEL_LEN
    top_n = min(NSA_TOP_N, nsel)
    ratio = NSA_SEL_LEN // NSA_CMP_STRIDE
    overlap = np.convolve(np.ones(ratio), np.ones(NSA_CMP_LEN // NSA_CMP_STRIDE)).tolist()
    n_left = (NSA_CMP_LEN - NSA_CMP_STRIDE) // NSA_CMP_STRIDE
    n_right = len(overlap) + ratio * (nsel - 1) - nc - n_left
    ks_blk = k_slc.reshape(B, nsel, NSA_SEL_LEN, dh)
    vs_blk = v_slc.reshape(B, nsel, NSA_SEL_LEN, dh)
    kw_pad = jnp.pad(k_win, ((0, 0), (NSA_WINDOW, 0), (0, 0)))
    vw_pad = jnp.pad(v_win, ((0, 0), (NSA_WINDOW, 0), (0, 0)))
    blk = jnp.arange(nsel)
    bidx = jnp.arange(B)[:, None, None]
    lpos = jnp.arange(NSA_SEL_LEN)
    nkeys_sel = top_n * NSA_SEL_LEN

    def block(i):
        q0 = i * Q_BLOCK
        qb = lax.dynamic_slice_in_dim(q, q0, Q_BLOCK, axis=1)
        qpos = q0 + jnp.arange(Q_BLOCK)
        dc = qpos[:, None] - cend[None, :]
        zc = jnp.einsum('bqhd,bnd->bhqn', qb, kc).astype(jnp.float32) * scale - slopes[:, None, None] * dc
        pc = masked_softmax(zc, dc >= 0)
        o_cmp = jnp.einsum('bhqn,bnd->bqhd', pc.astype(vc.dtype), vc)
        pg = jnp.pad(jnp.sum(pc, axis=1), ((0, 0), (0, 0), (n_left, n_right)))
        imp = sum(c * pg[..., o:o + ratio * nsel:ratio] for o, c in enumerate(overlap))
        cur = qpos // NSA_SEL_LEN
        forced = (blk[None, :] == 0) | (blk[None, :] == cur[:, None]) | (blk[None, :] == cur[:, None] - 1)
        future = blk[None, :] > cur[:, None]
        imp = jnp.where(future, -jnp.inf, jnp.where(forced, jnp.inf, imp))
        _, sel = lax.top_k(imp, top_n)
        ksel = ks_blk[bidx, sel]
        vsel = vs_blk[bidx, sel]
        spos = sel[..., None] * NSA_SEL_LEN + lpos
        ds = qpos[None, None, :, None, None] - spos[:, None]
        zs = jnp.einsum('bqhd,bqnld->bhqnl', qb, ksel).astype(jnp.float32) * scale - slopes[:, None, None, None] * ds
        ps = masked_softmax(zs.reshape(B, H, Q_BLOCK, nkeys_sel), (ds >= 0).reshape(B, 1, Q_BLOCK, nkeys_sel))
        o_slc = jnp.einsum('bhqnl,bqnld->bqhd', ps.reshape(B, H, Q_BLOCK, top_n, NSA_SEL_LEN).astype(vsel.dtype), vsel)
        kw = lax.dynamic_slice_in_dim(kw_pad, q0, Q_BLOCK + NSA_WINDOW, axis=1)
        vw = lax.dynamic_slice_in_dim(vw_pad, q0, Q_BLOCK + NSA_WINDOW, axis=1)
        wpos = q0 - NSA_WINDOW + jnp.arange(Q_BLOCK + NSA_WINDOW)
        dw = qpos[:, None] - wpos[None, :]
        mw = (dw >= 0) & (dw < NSA_WINDOW) & (wpos[None, :] >= 0)
        zw = jnp.einsum('bqhd,bkd->bhqk', qb, kw).astype(jnp.float32) * scale - slopes[:, None, None] * dw
        o_win = jnp.einsum('bhqk,bkd->bqhd', masked_softmax(zw, mw).astype(vw.dtype), vw)
        g = lax.dynamic_slice_in_dim(gates, q0, Q_BLOCK, axis=1)
        return g[..., 0:1] * o_cmp + g[..., 1:2] * o_slc + g[..., 2:3] * o_win

    out = lax.map(block, jnp.arange(S // Q_BLOCK))
    return jnp.swapaxes(out, 0, 1).reshape(B, S, H * dh)

def moba_attention(q, k, v, slopes):
    B, S, H, dh = q.shape
    scale = dh ** -0.5
    nb = -(-S // MOBA_BLOCK)
    pad = nb * MOBA_BLOCK - S
    kp = jnp.pad(k, ((0, 0), (0, pad), (0, 0)))
    vp = jnp.pad(v, ((0, 0), (0, pad), (0, 0)))
    k_blk = kp.reshape(B, nb, MOBA_BLOCK, dh)
    v_blk = vp.reshape(B, nb, MOBA_BLOCK, dh)
    k_mean = jnp.mean(k_blk, axis=2)
    top_k = min(MOBA_TOPK, nb)
    bidx = jnp.arange(B)[:, None, None]
    blk = jnp.arange(nb)
    lpos = jnp.arange(MOBA_BLOCK)
    nkeys_sel = top_k * MOBA_BLOCK

    def block(i):
        q0 = i * Q_BLOCK
        qb = lax.dynamic_slice_in_dim(q, q0, Q_BLOCK, axis=1)
        qpos = q0 + jnp.arange(Q_BLOCK)
        cur = q0 // MOBA_BLOCK
        sg = jnp.einsum('bqhd,bnd->bqn', qb, k_mean).astype(jnp.float32)
        sg = jnp.where(blk < cur, sg, -jnp.inf)
        gv, sel = lax.top_k(sg, top_k)
        ksel = k_blk[bidx, sel]
        vsel = v_blk[bidx, sel]
        spos = sel[..., None] * MOBA_BLOCK + lpos
        ds = qpos[None, None, :, None, None] - spos[:, None]
        zs = jnp.einsum('bqhd,bqnld->bhqnl', qb, ksel).astype(jnp.float32) * scale - slopes[:, None, None, None] * ds
        ms = jnp.broadcast_to(jnp.isfinite(gv)[:, None, :, :, None], zs.shape)
        ko = lax.dynamic_slice_in_dim(kp, cur * MOBA_BLOCK, MOBA_BLOCK, axis=1)
        vo = lax.dynamic_slice_in_dim(vp, cur * MOBA_BLOCK, MOBA_BLOCK, axis=1)
        do = qpos[:, None] - (cur * MOBA_BLOCK + lpos)[None, :]
        zo = jnp.einsum('bqhd,bld->bhql', qb, ko).astype(jnp.float32) * scale - slopes[:, None, None] * do
        mo = jnp.broadcast_to(do >= 0, zo.shape)
        z = jnp.concatenate([zs.reshape(B, H, Q_BLOCK, nkeys_sel), zo], axis=-1)
        m = jnp.concatenate([ms.reshape(B, H, Q_BLOCK, nkeys_sel), mo], axis=-1)
        p = masked_softmax(z, m).astype(v.dtype)
        ps = p[..., :nkeys_sel].reshape(B, H, Q_BLOCK, top_k, MOBA_BLOCK)
        po = p[..., nkeys_sel:]
        return jnp.einsum('bhqnl,bqnld->bqhd', ps, vsel) + jnp.einsum('bhql,bld->bqhd', po, vo)

    out = lax.map(block, jnp.arange(S // Q_BLOCK))
    return jnp.swapaxes(out, 0, 1).reshape(B, S, H * dh)

def peer_ffn(x, w_q, sub_k1, sub_k2, u_tab, v_tab):
    B, S, D = x.shape
    half = PEER_QDIM // 2
    xt = x.reshape(B * S // TOK_BLOCK, TOK_BLOCK, D)

    def block(xb):
        q = jnp.einsum('td,dhc->thc', xb, w_q)
        s1 = jnp.einsum('thc,hkc->thk', q[..., :half], sub_k1).astype(jnp.float32)
        s2 = jnp.einsum('thc,hkc->thk', q[..., half:], sub_k2).astype(jnp.float32)
        v1, i1 = lax.top_k(s1, PEER_TOPK)
        v2, i2 = lax.top_k(s2, PEER_TOPK)
        cand = (v1[..., :, None] + v2[..., None, :]).reshape(TOK_BLOCK, PEER_HEADS, PEER_TOPK * PEER_TOPK)
        cidx = (i1[..., :, None] * PEER_NKEYS + i2[..., None, :]).reshape(TOK_BLOCK, PEER_HEADS, PEER_TOPK * PEER_TOPK)
        top, pos = lax.top_k(cand, PEER_TOPK)
        idx = jnp.take_along_axis(cidx, pos, axis=-1)
        g = jax.nn.softmax(top, axis=-1)
        act = jax.nn.gelu(jnp.einsum('thkd,td->thk', u_tab[idx], xb).astype(jnp.float32))
        return jnp.einsum('thk,thkd->td', (g * act).astype(v_tab.dtype), v_tab[idx])

    return lax.map(block, xt).reshape(B, S, D)

def hybrid_layer(x, w_in, nsa_pe_k, nsa_pe_v, nsa_w_ck, nsa_w_cv, w_br_sb, w_br_nsa, w_br_moba, w_out, ln1_g, ln1_b, peer_wq, peer_k1, peer_k2, peer_u, peer_v, ln2_g, ln2_b, nsa_slopes, moba_slopes):
    B, S, D = x.shape
    split_points = np.cumsum(IN_WIDTHS)[:-1].tolist()
    (sb_q, sb_k, sb_v, nsa_q, ck, cv, sk, sv, wk, wv, nsa_g, mb_q, mb_k, mb_v, merge_g) = jnp.split(x @ w_in, split_points, axis=-1)
    heads = lambda t, h: t.reshape(B, S, h, HEAD_DIM)
    bhsd = lambda t, h: jnp.transpose(heads(t, h), (0, 2, 1, 3))
    o_sb = stick_breaking_attention(bhsd(sb_q, SB_HEADS), bhsd(sb_k, SB_HEADS), bhsd(sb_v, SB_HEADS))
    o_nsa = nsa_attention(heads(nsa_q, NSA_HEADS), ck, cv, sk, sv, wk, wv, jax.nn.sigmoid(nsa_g).reshape(B, S, NSA_HEADS, 3), nsa_pe_k, nsa_pe_v, nsa_w_ck, nsa_w_cv, nsa_slopes)
    o_moba = moba_attention(heads(mb_q, MOBA_HEADS), mb_k, mb_v, moba_slopes)
    g = jax.nn.sigmoid(merge_g).reshape(B, S, N_BRANCHES, D)
    mix = g[:, :, 0] * (o_sb @ w_br_sb) + g[:, :, 1] * (o_nsa @ w_br_nsa) + g[:, :, 2] * (o_moba @ w_br_moba)
    x = layer_norm(DEEPNORM_ALPHA * x + mix @ w_out, ln1_g, ln1_b)
    return layer_norm(DEEPNORM_ALPHA * x + peer_ffn(x, peer_wq, peer_k1, peer_k2, peer_u, peer_v), ln2_g, ln2_b)

def setup_inputs(seed: int = 0) -> dict:
    key = jax.random.key(seed)
    ks = jax.random.split(key, 20)
    L, D = DEPTH, D_MODEL
    nrm = lambda k, shape, s: s * jax.random.normal(k, shape, jnp.float32)
    return {
        'x': nrm(ks[0], (BATCH, SEQ, D), 1.0),
        'w_in': nrm(ks[1], (L, D, IN_WIDTH), D ** -0.5),
        'nsa_pe_k': nrm(ks[2], (L, NSA_CMP_LEN, HEAD_DIM), 0.02),
        'nsa_pe_v': nrm(ks[3], (L, NSA_CMP_LEN, HEAD_DIM), 0.02),
        'nsa_w_ck': nrm(ks[4], (L, NSA_CMP_LEN * HEAD_DIM, HEAD_DIM), (NSA_CMP_LEN * HEAD_DIM) ** -0.5),
        'nsa_w_cv': nrm(ks[5], (L, NSA_CMP_LEN * HEAD_DIM, HEAD_DIM), (NSA_CMP_LEN * HEAD_DIM) ** -0.5),
        'w_br_sb': nrm(ks[6], (L, SB_W, D), DEEPNORM_BETA * SB_W ** -0.5),
        'w_br_nsa': nrm(ks[7], (L, NSA_W, D), DEEPNORM_BETA * NSA_W ** -0.5),
        'w_br_moba': nrm(ks[8], (L, MOBA_W, D), DEEPNORM_BETA * MOBA_W ** -0.5),
        'w_out': nrm(ks[9], (L, D, D), DEEPNORM_BETA * D ** -0.5),
        'ln1_g': 1.0 + nrm(ks[10], (L, D), 0.01),
        'ln1_b': nrm(ks[11], (L, D), 0.01),
        'peer_wq': nrm(ks[12], (L, D, PEER_HEADS, PEER_QDIM), D ** -0.5),
        'peer_k1': nrm(ks[13], (L, PEER_HEADS, PEER_NKEYS, PEER_QDIM // 2), (PEER_QDIM // 2) ** -0.5),
        'peer_k2': nrm(ks[14], (L, PEER_HEADS, PEER_NKEYS, PEER_QDIM // 2), (PEER_QDIM // 2) ** -0.5),
        'peer_u': nrm(ks[15], (L, PEER_N_EXPERTS, D), D ** -0.5),
        'peer_v': nrm(ks[16], (L, PEER_N_EXPERTS, D), DEEPNORM_BETA * PEER_HEADS ** -0.5),
        'ln2_g': 1.0 + nrm(ks[17], (L, D), 0.01),
        'ln2_b': nrm(ks[18], (L, D), 0.01),
    }

def reference(x, w_in, nsa_pe_k, nsa_pe_v, nsa_w_ck, nsa_w_cv, w_br_sb, w_br_nsa, w_br_moba, w_out, ln1_g, ln1_b, peer_wq, peer_k1, peer_k2, peer_u, peer_v, ln2_g, ln2_b):
    slopes = alibi_slopes(NSA_HEADS + MOBA_HEADS)
    nsa_slopes = slopes[0::2]
    moba_slopes = slopes[1::2]
    for l in range(DEPTH):
        x = hybrid_layer(x, w_in[l], nsa_pe_k[l], nsa_pe_v[l], nsa_w_ck[l], nsa_w_cv[l], w_br_sb[l], w_br_nsa[l], w_br_moba[l], w_out[l], ln1_g[l], ln1_b[l], peer_wq[l], peer_k1[l], peer_k2[l], peer_u[l], peer_v[l], ln2_g[l], ln2_b[l], nsa_slopes, moba_slopes)
    return x


_drawn_inputs = setup_inputs


def setup_inputs(seed=0):
    import zlib

    import numpy as np

    out = dict(_drawn_inputs(seed))
    spreads = {}
    factors = {'nsa_pe_k': 64.0, 'nsa_pe_v': 26.853, 'ln2_g': 9.409, 'ln2_b': 9.689}
    for name, (base, spread) in spreads.items():
        noise = np.random.default_rng([zlib.crc32(name.encode()), seed]).standard_normal(out[name].shape)
        drawn = base * np.exp(spread * noise) if base else spread * noise
        out[name] = __import__('jax').numpy.asarray(drawn.astype(out[name].dtype))
    for name, factor in factors.items():
        out[name] = (out[name] * factor).astype(out[name].dtype)
    return out
```

```python
from contextlib import ExitStack

import concourse.bass as bass
from concourse import mybir

F32 = mybir.dt.float32
I32 = mybir.dt.int32
U32 = mybir.dt.uint32
ALU = mybir.AluOpType
ACT = mybir.ActivationFunctionType
AX_X = mybir.AxisListType.X

P = 128
D = 1024
KC = D // P
SEQ = 1024
DEPTH = 2
HD = 32
NH = 4
CMP_STRIDE, CMP_LEN = 16, 32
NCMP = SEQ // CMP_STRIDE - 1
NSEL = SEQ // 64
NKEYS, TOPK, PH = 128, 8, 4
NEXP = PH * TOPK
N_EXPERTS = NKEYS * NKEYS
ALPHA = (2.0 * DEPTH) ** 0.25
LN_EPS = 1e-5
BIG = 1e30
NSA_SLOPES = [2.0 ** -(2 * h + 1) for h in range(NH)]
MOBA_SLOPES = [2.0 ** -(2 * h + 2) for h in range(NH)]

GT = 4
GW = GT * P
NG = DEPTH * SEQ // GW
TILES = SEQ // P
GATHER_SLOTS = 6
STEPS = 2 * GT * NEXP
NITEM = 13
ITEM = 9 * 512

C_ID, C_NTRI, C_NONE, C_NEG, C_PAST = 0, 128, 256, 384, 512
C_T = 640
C_W = C_T + 1024
C_C = C_W + 640
C_F = C_C + 63
C_IOTA = C_F + 30
C_QS = C_IOTA + 64
C_END = C_QS + 2


def constants():
    import numpy as np

    c = np.zeros((P, C_END), np.float32)
    p = np.arange(P)[:, None]
    x = np.arange(P)[None, :]
    c[:, C_ID:C_ID + P] = p == x
    c[:, C_NTRI:C_NTRI + P] = np.where(p >= x, -1.0, 0.0)
    c[:, C_NONE:C_NONE + P] = -1.0
    c[:, C_NEG:C_NEG + P] = np.where(p < x, 0.0, -BIG)
    c[:, C_PAST:C_PAST + P] = p < x
    d = p - (np.arange(1024)[None, :] - 896)
    c[:, C_T:C_T + 1024] = np.where(d >= 0, d, BIG)
    d = p - (np.arange(640)[None, :] - 512)
    c[:, C_W:C_W + 640] = np.where((d >= 0) & (d < 512), d, BIG)
    d = p - CMP_STRIDE * (np.arange(63)[None, :] - 56) - (CMP_LEN - 1)
    c[:, C_C:C_C + 63] = np.where(d >= 0, d, BIG)
    r = np.arange(30)[None, :] - 14
    cur = p // 64
    c[:, C_F:C_F + 30] = np.where(r > cur, -BIG, np.where(r >= cur - 1, BIG, 0.0))
    c[:, C_IOTA:C_IOTA + 64] = np.arange(64)[None, :]
    h = np.arange(P) // HD
    c[:, C_QS] = -(HD ** -0.5) / np.array(NSA_SLOPES)[h]
    c[:, C_QS + 1] = -(HD ** -0.5) / np.array(MOBA_SLOPES)[h]
    return c


def sb_before(T):
    i = T % TILES
    return (T // TILES) * (TILES * (TILES + 1) // 2) + i * (i + 1) // 2


def group_points(g):
    pts = [("proj", n, 10.0) for n in range(6)]
    for t in range(GT):
        i = (g * GT + t) % TILES
        for n in range(12):
            pts.append(("soft", t * 12 + n, 0.4 * (min(i + 1, 5) if n < 4 else i + 1)))
        for m in range(i + 1):
            pts.append(("sb", (t, m), 3.1))
    pts += [("merge", k, 7.7) for k in range(24)]
    pts += [("ln1", t, 17.0) for t in range(GT)]
    pts += [("query", j, 6.9) for j in range(8)]
    pts += [("route", t, 6.0) for t in range(GT)]
    return pts


def shares(g):
    pts = group_points(g)
    factor = {"proj": 1.3, "soft": 1.1, "sb": 1.0, "merge": 1.0, "ln1": 0.7, "query": 1.0, "route": 0.0}
    pts = [(kind, n, w * factor[kind]) for kind, n, w in pts]
    whole = sum(w for _, _, w in pts)
    out, at, last = {}, 0.0, 0
    for kind, n, w in pts:
        at += w
        to = round(STEPS * at / whole)
        if kind == "ln1":
            to = max(to, GT * NEXP + NEXP * n + 1)
        to = max(to, last)
        out[(kind, n)] = range(last, to)
        last = to
    return out


def hybrid_layers(nc, consts, x_in, w_attn_a, w_attn_b, w_cmp, pe_cmp, w_merge, w_out, ln1, w_query,
                  keys, tab_u, tab_v, ln2, out):
    x_mid = nc.dram_tensor("x_mid", [SEQ, D], F32, kind="Internal").ap()
    ctx = ExitStack()
    with ctx:
        def sb(name, shape, dt=F32):
            return ctx.enter_context(nc.sbuf_tensor(name, shape, dt))

        def sem(name):
            return ctx.enter_context(nc.semaphore(name))

        cst = sb("cst", [P, C_END])
        xT = sb("xT", [P, KC, GW])
        x_row = sb("x_row", [P, 2, D])
        x1 = sb("x1", [P, GT, D])
        y = sb("y", [P, D])
        rows = sb("rows", [P, GATHER_SLOTS, D])
        wring = sb("wring", [P, 2, ITEM])
        q_sb = sb("q_sb", [P, GW])
        q_nsa = sb("q_nsa", [P, GW])
        q_moba = sb("q_moba", [P, GW])
        k_sb = sb("k_sb", [P, SEQ])
        k_slc = sb("k_slc", [P, SEQ])
        k_win = sb("k_win", [P, SEQ])
        k_moba = sb("k_moba", [P, SEQ])
        ck_sh = sb("ck_sh", [P, SEQ])
        cv_sh = sb("cv_sh", [P, SEQ])
        kc_T = sb("kc_T", [P, NH, 64])
        q_heads = sb("q_heads", [P, NH, P])
        vc = sb("vc", [64, HD])
        vals = sb("vals", [P, TILES, 236])
        gate_e = sb("gate_e", [P, GT, 12])
        gates = sb("gates", [P, GT, 12])
        scratch = sb("scratch", [P, 2, 4096])
        ln1_gb = sb("ln1_gb", [P, 2, D])
        ln2_gb = sb("ln2_gb", [P, 2, D])
        row_buf = sb("row_buf", [P, 512])
        zc = sb("zc", [P, NH, 64])
        den = sb("den", [P, 2, 16])
        rden = sb("rden", [P, 16])
        negm = sb("negm", [P, 4])
        negm_c = sb("negm_c", [P, NH])
        pg = sb("pg", [P, 66])
        imp = sb("imp", [P, 3, NSEL])
        top8 = sb("top8", [P, 8])
        stats = sb("stats", [P, 2, 6])
        mv = sb("mv", [P, 8])
        stats2 = sb("stats2", [P, 2, 6])
        mv2 = sb("mv2", [P, 8])
        v8 = sb("v8", [P, 2, 8])
        i8 = sb("i8", [P, 2, 8], U32)
        i8f = sb("i8f", [P, 2, 8])
        cand = sb("cand", [P, 64])
        cidx = sb("cidx", [P, 64])
        pos = sb("pos", [P, 8], U32)
        posf = sb("posf", [P, 8])
        top = sb("top", [P, PH, TOPK])
        topsum = sb("topsum", [P, PH])
        idxf = sb("idxf", [P, NEXP])
        idx = sb("idx", [P, 2 * GT, NEXP], I32)
        gw = sb("gw", [P, 2 * GT, NEXP])
        dots = sb("dots", [P, GT, NEXP])
        gel = sb("gel", [P, NEXP])
        wts = sb("wts", [P, GT, NEXP])

        zb = [scratch[:, 0, 1024 * b:1024 * (b + 1)] for b in range(2)]
        pT_sb = [scratch[:, 0, 2048 + 1024 * b:2048 + 1024 * (b + 1)] for b in range(2)]
        s2 = scratch[:, 1, :]
        lbuf = [s2[:, 512 * b:512 * (b + 1)] for b in range(2)]
        spb = [s2[:, 1024 + 512 * b:1024 + 512 * (b + 1)] for b in range(2)]
        wb = [s2[:, 2048 + 512 * b:2048 + 512 * (b + 1)] for b in range(2)]
        accb = [s2[:, 3072 + 512 * b:3072 + 512 * (b + 1)] for b in range(2)]
        mix = scratch[:, 0, :].rearrange("p (t n) -> p t n", t=GT)
        qp_T = scratch[:, 1, :].rearrange("p (c n) -> p c n", c=8)
        gate_buf = [s2[:, 512 * b:512 * (b + 1)] for b in range(4)]
        o_row = row_buf[:, 0:384]
        eqbuf = row_buf[:, :]
        selT = s2[:, 2048:3072]
        pc_T = selT

        ps = ctx.enter_context(nc.psum_tensor("ps", [P, 8, 512], F32))

        def bank(b):
            return ps[:, b, :]

        def pair(b):
            return ps[:, b:b + 2, :].rearrange("p a n -> p (a n)")

        ident = cst[:, C_ID:C_ID + P]
        item_landed = [sem("item_landed0"), sem("item_landed1")]
        row_landed = [sem("x_row_landed0"), sem("x_row_landed1")]
        expert_landed = [sem(f"expert_landed{n}") for n in range(GATHER_SLOTS)]
        names = """const_landed ln1_landed ln2_landed item_used x_turned resid_used xT_copied proj_done
            proj_copied v_done v_copied cmp_done cmp_copied gate_exp gates_ready zc_done zc_scored zc_exp
            pc_turned pc_copied z_done scored probs p_turned p_copied pv_done zsb_done softplus sp_ready
            acc_ready sb_summed sb_w sb_pv o_rows_v o_rows_a o_turned oT_copied merge_done gate_e_done
            merged mix_turned mixT_copied out_done out_added var_ready rstd ln1_done x1_turned
            x1T_copied query_done query_copied scores_done topk_ready top_exp routed idx_ready
            row_used gelu_in gelu_exp var2_ready rstd2 y_ready y_stored q_spread zeros_set gate_arg gate_sig dve_chain act_chain""".split()
        s = {n: sem(n) for n in names}

        (const_landed, ln1_landed, ln2_landed, item_used, x_turned, resid_used, xT_copied, proj_done,
         proj_copied, v_done, v_copied, cmp_done, cmp_copied, gate_exp, gates_ready, zc_done, zc_scored,
         zc_exp, pc_turned, pc_copied, z_done, scored, probs, p_turned, p_copied, pv_done, zsb_done,
         softplus, sp_ready, acc_ready, sb_summed, sb_w, sb_pv, o_rows_v, o_rows_a, o_turned, oT_copied,
         merge_done, gate_e_done, merged, mix_turned, mixT_copied, out_done, out_added, var_ready, rstd,
         ln1_done, x1_turned, x1T_copied, query_done, query_copied, scores_done, topk_ready, top_exp,
         routed, idx_ready, row_used, gelu_in, gelu_exp, var2_ready, rstd2, y_ready, y_stored,
         q_spread, zeros_set, gate_arg, gate_sig, dve_chain, act_chain) = [s[n] for n in names]

        def blocks(n, i):
            nb = min(i + 1, 5) if n < 4 else i + 1
            return i + 1 - nb, nb

        def segment_freed(eng, g, r):
            if r < 0:
                eng.wait_ge(merged, 24 * g + 24 + r + 1)
            elif r < 8:
                eng.wait_ge(mixT_copied, 8 * g + r + 1)
            elif r < 16:
                eng.wait_ge(out_added, 8 * g + r - 8 + 1)
            elif r < 24:
                eng.wait_ge(x1T_copied, 8 * g + r - 16 + 1)
            else:
                eng.wait_ge(query_copied, 8 * g + r - 24 + 1)

        block = ctx.enter_context(nc.Block())

        @block.sync
        def _(sp):
            sp.dma_start(cst[:, :], consts).then_inc(const_landed, 16)
            for g in range(NG):
                layer, half = g // 2, g % 2
                if half == 0:
                    if g > 0:
                        sp.wait_ge(ln1_done, GT * g)
                    sp.dma_start(ln1_gb[:, :, :], ln1[layer].partition_broadcast(P)).then_inc(ln1_landed, 16)

                def item(k):
                    n = NITEM * g + k
                    if n >= 2:
                        sp.wait_ge(item_used, n - 1)
                    src = ([w_attn_a[layer], w_attn_b[layer]] + [w_merge[layer, c] for c in range(6)]
                           + [w_out[layer, h] for h in range(2)] + [w_query[layer, h] for h in range(2)]
                           + [keys[layer]])[k]
                    sp.dma_start(wring[:, n % 2, 0:src.shape[1]], src).then_inc(item_landed[n % 2], 16)

                def x_rows(t, residual):
                    m = 2 * GT * g + GT * residual + t
                    T = GT * g + t
                    if layer > 0 and not residual:
                        sp.wait_ge(y_stored, 16 * (T - TILES + 1))
                    if m >= 2:
                        if t >= 2:
                            if residual:
                                sp.wait_ge(resid_used, T - 1)
                            else:
                                sp.wait_ge(x_turned, 2 * (T - 1))
                        elif residual:
                            sp.wait_ge(x_turned, 2 * (GT * g + t + 3))
                        else:
                            sp.wait_ge(resid_used, GT * (g - 1) + t + 3)
                    src = (x_in if layer == 0 else x_mid)[(T % TILES) * P:(T % TILES + 1) * P, :]
                    sp.dma_start(x_row[:, m % 2, :], src).then_inc(row_landed[m % 2], 16)

                item(0)
                item(1)
                if g == 0 or g == NG // DEPTH + 1:
                    if g > 0:
                        sp.wait_ge(y_ready, TILES)
                    sp.dma_start(ln2_gb[:, :, :], ln2[layer].partition_broadcast(P)).then_inc(ln2_landed, 16)
                for t in range(GT):
                    x_rows(t, 0)
                for k in range(2, 9):
                    item(k)
                x_rows(0, 1)
                x_rows(1, 1)
                item(9)
                x_rows(2, 1)
                x_rows(3, 1)
                for k in range(10, NITEM):
                    item(k)

        @block.gpsimd
        def _(pool):
            for g in range(NG):
                for st in range(STEPS):
                    n = STEPS * g + st
                    t, e = (st % (GT * NEXP)) // NEXP, st % NEXP
                    if st < GT * NEXP and e == 0:
                        pool.wait_ge(idx_ready, GT * g + t + 1)
                    if n >= GATHER_SLOTS:
                        pool.wait_ge(row_used, n - GATHER_SLOTS + 1)
                    pool.indirect_dma_start(
                        rows[:, n % GATHER_SLOTS, :], None, tab_u if st < GT * NEXP else tab_v,
                        bass.IndirectOffsetOnAxis(ap=idx[:, GT * (g % 2) + t, e:e + 1], axis=0),
                    ).then_inc(expert_landed[n % GATHER_SLOTS], 16)

        @block.tensor
        def _(pe):
            pe.wait_ge(const_landed, 16)

            def slot(g, k):
                n = NITEM * g + k
                pe.wait_ge(item_landed[n % 2], 16 * (n // 2 + 1))
                return wring[:, n % 2, :]

            def turn(dst, src):
                return pe.matmul(dst, src, ident[0:src.shape[0], 0:src.shape[0]], is_transpose=True,
                                 start=True, stop=True)

            for g in range(NG):
                layer, half = g // 2, g % 2
                for t in range(GT):
                    T = GT * g + t
                    m = 2 * GT * g + t
                    pe.wait_ge(row_landed[m % 2], 16 * (m // 2 + 1))
                    for hf in range(2):
                        j = 2 * T + hf
                        if j % 8 >= 4:
                            pe.wait_ge(xT_copied, j - 3)
                        elif g > 0:
                            pe.wait_ge(query_copied, 8 * g)
                        for c in range(4):
                            kc = 4 * hf + c
                            mm = turn(bank(j % 4)[:, P * c:P * (c + 1)], x_row[:, m % 2, P * kc:P * (kc + 1)])
                        mm.then_inc(x_turned, 1)
                pe.wait_ge(xT_copied, 8 * (g + 1))
                wa = slot(g, 0)[:, 0:KC * 512].rearrange("p (c n) -> p c n", c=KC)
                for j in range(6):
                    if j == 4:
                        wb_ = slot(g, 1)[:, 0:KC * 396].rearrange("p (c n) -> p c n", c=KC)
                    if j >= 4:
                        pe.wait_ge(proj_copied, 6 * g + j - 3)
                    for c in range(KC):
                        w = wa[:, c, P * j:P * (j + 1)] if j < 4 else wb_[:, c, 0:P] if j == 4 else wb_[:, c, P:P + HD]
                        mm = pe.matmul(bank(j % 4)[0:w.shape[1], :], w, xT[:, c, :], start=(c == 0), stop=(c == KC - 1))
                    mm.then_inc(proj_done, 1)
                    if j == 3:
                        pe.wait_ge(proj_done, 6 * g + 4)
                        pe.nop().then_inc(item_used, 1)
                if g > 0:
                    pe.wait_ge(routed, GT * g)
                for t in range(GT):
                    if t >= 2:
                        pe.wait_ge(v_copied, GT * g + t - 1)
                    for c in range(KC):
                        mm = pe.matmul(bank(4 + t % 2)[:, 0:236], xT[:, c, P * t:P * (t + 1)], wb_[:, c, 160:396],
                                       start=(c == 0), stop=(c == KC - 1))
                    mm.then_inc(v_done, 1)
                pe.wait_ge(proj_copied, 6 * g + 6)
                nc_ = 31 if half == 0 else NCMP
                extra = wring[:, (NITEM * g + 1) % 2, KC * 396:]
                wk_c = extra[:, 0:KC * HD].rearrange("p (c n) -> p c n", c=KC)
                wv_c = extra[:, KC * HD:2 * KC * HD].rearrange("p (c n) -> p c n", c=KC)
                pe_k = extra[:, 2 * KC * HD:2 * KC * HD + KC]
                pe_v = extra[:, 2 * KC * HD + KC:2 * KC * HD + 2 * KC]
                last_tok = CMP_STRIDE * (nc_ - 1) + 1
                for c in range(KC):
                    pe.matmul(bank(6)[0:HD, 0:nc_], wk_c[:, c, :], ck_sh[:, 4 * c:4 * c + last_tok:CMP_STRIDE],
                              start=(c == 0), stop=False)
                    mm = pe.matmul(bank(6)[0:HD, 0:nc_], wk_c[:, c, :], pe_k[:, c:c + 1].to_broadcast([P, nc_]),
                                   start=False, stop=(c == KC - 1))
                mm.then_inc(cmp_done, 1)
                for c in range(KC):
                    pe.matmul(bank(7)[0:nc_, 0:HD], cv_sh[:, 4 * c:4 * c + last_tok:CMP_STRIDE], wv_c[:, c, :],
                              start=(c == 0), stop=False)
                    mm = pe.matmul(bank(7)[0:nc_, 0:HD], pe_v[:, c:c + 1].to_broadcast([P, nc_]), wv_c[:, c, :],
                                   start=False, stop=(c == KC - 1))
                mm.then_inc(cmp_done, 1)
                pe.wait_ge(cmp_done, 2 * (g + 1))
                pe.nop().then_inc(item_used, 1)
                pe.wait_ge(v_copied, GT * (g + 1))
                pe.wait_ge(cmp_copied, 2 * (g + 1))
                for t in range(GT):
                    T = GT * g + t
                    i = T % TILES
                    nct = 8 * i + 7
                    tok = slice(P * t, P * (t + 1))
                    obank = bank(6 + T % 2)

                    def z_unit(n):
                        N = 12 * T + n
                        if N >= 2 and n >= 2:
                            pe.wait_ge(scored, N - 1)
                        k0, nb = blocks(n, i)
                        h = n % NH
                        r = slice(HD * h, HD * (h + 1))
                        q, k = ((q_nsa, k_win), (q_moba, k_moba), (q_nsa, k_slc))[n // NH]
                        z = pair(2 * (N % 2))
                        for a in range(0, nb * P, 512):
                            w = min(512, nb * P - a)
                            mm = pe.matmul(z[:, a:a + w], q[r, tok], k[r, k0 * P + a:k0 * P + a + w],
                                           start=True, stop=True, skip_group_check=True)
                        mm.then_inc(z_done, 1)

                    def p_turn(n):
                        N = 12 * T + n
                        pe.wait_ge(probs, N + 1)
                        if N >= 1:
                            pe.wait_ge(p_copied, N)
                        _, nb = blocks(n, i)
                        for b in range(nb):
                            mm = turn(bank(4 + b // 4)[:, P * (b % 4):P * (b % 4 + 1)], zb[N % 2][:, P * b:P * (b + 1)])
                        mm.then_inc(p_turned, 1)

                    def pv(n):
                        N = 12 * T + n
                        pe.wait_ge(p_copied, N + 1)
                        k0, nb = blocks(n, i)
                        h = n % NH
                        col = (128, 256, 384)[n // NH] + HD * h
                        vcol = (160, 192, 128)[n // NH]
                        for b in range(nb):
                            mm = pe.matmul(obank[:, col:col + HD], pT_sb[N % 2][:, P * b:P * (b + 1)],
                                           vals[:, k0 + b, vcol:vcol + HD], start=False, stop=(b == nb - 1),
                                           skip_group_check=True)
                        mm.then_inc(pv_done, 1)

                    if T >= 1 and t >= 1:
                        pe.wait_ge(sb_w, sb_before(T))
                        pe.wait_ge(oT_copied, T)
                    if T >= 2:
                        pe.wait_ge(o_rows_v, T - 1)
                    pe.matmul(bank(4)[:, 0:NH * nct].rearrange("p (h n) -> p h n", h=NH), q_nsa[:, tok],
                              kc_T[:, :, 0:nct], start=True, stop=True).then_inc(zc_done, 1)
                    z_unit(0)
                    z_unit(1)
                    pe.wait_ge(zc_exp, T + 1)
                    for h in range(NH):
                        mm = turn(bank(5)[0:nct, P * h:P * (h + 1)], zc[:, h, 0:nct])
                    mm.then_inc(pc_turned, 1)
                    pe.wait_ge(pc_copied, T + 1)
                    for h in range(NH):
                        mm = pe.matmul(obank[:, HD * h:HD * (h + 1)], pc_T[0:nct, P * h:P * (h + 1)], vc[0:nct, :],
                                       start=(h == 0), stop=True, skip_group_check=True)
                    mm.then_inc(pv_done, 1) if False else None
                    for n in range(12):
                        if n + 2 < 12:
                            z_unit(n + 2)
                        p_turn(n)
                        if n >= 1:
                            pv(n - 1)
                    pv(11)

                    def z_sb(m):
                        M = sb_before(T) + m
                        if m < 4:
                            pe.wait_ge(scored, 12 * (T + 1))
                        else:
                            pe.wait_ge(sb_w, M - 3)
                        kb = i - m
                        if m == 0:
                            pe.wait_ge(q_spread, T + 1)
                        pe.matmul(bank(M % 4), k_sb[:, P * kb:P * (kb + 1)], q_heads[:, :, :].rearrange("p h n -> p (h n)"),
                                  start=True, stop=True, skip_group_check=True).then_inc(zsb_done, 1)

                    def suffix(m):
                        M = sb_before(T) + m
                        pe.wait_ge(sp_ready, M + 1)
                        if m == 0:
                            pe.matmul(bank(M % 4).rearrange("p (h q) -> p h q", h=NH), ident,
                                      cst[:, C_NEG:C_NEG + P].unsqueeze(1).to_broadcast([P, NH, P]),
                                      start=False, stop=True, skip_group_check=True)
                        if m == 1:
                            pe.matmul(bank(M % 4), cst[:, C_NONE:C_NONE + P], spb[(M - 1) % 2],
                                      start=False, stop=True, skip_group_check=True)
                        if m >= 2:
                            pe.wait_ge(acc_ready, M)
                            pe.matmul(bank(M % 4), cst[:, C_NONE:C_NONE + P], accb[M % 2],
                                      start=False, stop=True, skip_group_check=True)
                        pe.matmul(bank(M % 4), cst[:, C_NTRI:C_NTRI + P], spb[M % 2],
                                  start=False, stop=True, skip_group_check=True).then_inc(sb_summed, 1)

                    def pv_sb(m):
                        M = sb_before(T) + m
                        pe.wait_ge(sb_w, M + 1)
                        if m == 0:
                            pe.wait_ge(p_copied, 12 * (T + 1))
                        for h in range(NH):
                            mm = pe.matmul(bank(5)[:, HD * h:HD * (h + 1)], wb[M % 2][:, P * h:P * (h + 1)],
                                           vals[:, i - m, HD * h:HD * (h + 1)], start=(m == 0 and h == 0), stop=(m == i),
                                           skip_group_check=True)
                        mm.then_inc(sb_pv, 1)

                    z_sb(0)
                    if i >= 1:
                        z_sb(1)
                    for m in range(i + 1):
                        if m + 2 <= i:
                            z_sb(m + 2)
                        suffix(m)
                        if m >= 1:
                            pv_sb(m - 1)
                    pv_sb(i)
                    pe.wait_ge(o_rows_v, T + 1)
                    pe.wait_ge(o_rows_a, T + 1)
                    for b in range(3):
                        mm = turn(bank(4)[:, P * b:P * (b + 1)], o_row[:, P * b:P * (b + 1)])
                    mm.then_inc(o_turned, 1)

                pe.wait_ge(oT_copied, GT * (g + 1))
                pe.wait_ge(sb_w, sb_before(GT * (g + 1)))
                for c6 in range(6):
                    w = slot(g, 2 + c6)
                    wg = w[:, 0:KC * 512].rearrange("p (c n) -> p c n", c=KC)
                    oT = (q_sb, q_nsa, q_moba)[c6 % 3]
                    for t in range(GT):
                        k = 24 * g + 4 * c6 + t
                        if k % 24 >= 4:
                            pe.wait_ge(merged, k - 3)
                        for c in range(KC):
                            pe.matmul(bank(k % 4), xT[:, c, P * t:P * (t + 1)], wg[:, c, :], start=(c == 0), stop=(c == KC - 1))
                        mm = pe.matmul(bank(4 + k % 4), oT[:, P * t:P * (t + 1)], w[:, KC * 512:], start=True, stop=True)
                        mm.then_inc(merge_done, 1)
                    pe.wait_ge(merge_done, 24 * g + 4 * (c6 + 1))
                    pe.nop().then_inc(item_used, 1)
                for r in range(8):
                    t = r // 2
                    segment_freed(pe, g, r - 4)
                    pe.wait_ge(merged, 24 * g + 20 + t + 1)
                    for c in range(4):
                        kc = 4 * (r % 2) + c
                        mm = turn(bank(r % 4)[:, P * c:P * (c + 1)], mix[:, t, P * kc:P * (kc + 1)])
                    mm.then_inc(mix_turned, 1)
                wo = [slot(g, 8 + h)[:, 0:KC * 512].rearrange("p (c n) -> p c n", c=KC) for h in range(2)]
                for r in range(8, 16):
                    t, h = (r - 8) // 2, r % 2
                    segment_freed(pe, g, r - 4)
                    pe.wait_ge(mixT_copied, 8 * g + 2 * t + 2)
                    for c in range(KC):
                        mm = pe.matmul(bank(r % 4), xT[:, c, P * t:P * (t + 1)], wo[h][:, c, :], start=(c == 0), stop=(c == KC - 1))
                    mm.then_inc(out_done, 1)
                pe.wait_ge(out_done, 8 * (g + 1))
                pe.nop().then_inc(item_used, 1)
                pe.nop().then_inc(item_used, 1)
                for r in range(16, 24):
                    t = (r - 16) // 2
                    segment_freed(pe, g, r - 4)
                    pe.wait_ge(ln1_done, GT * g + t + 1)
                    for c in range(4):
                        kc = 4 * (r % 2) + c
                        mm = turn(bank(r % 4)[:, P * c:P * (c + 1)], x1[:, t, P * kc:P * (kc + 1)])
                    mm.then_inc(x1_turned, 1)
                pe.wait_ge(x1T_copied, 8 * (g + 1))
                for r in range(24, 32):
                    j = r - 24
                    if j % 4 == 0:
                        wq = slot(g, 10 + j // 4)[:, 0:KC * 512].rearrange("p (c n) -> p c n", c=KC)
                    segment_freed(pe, g, r - 4)
                    for c in range(KC):
                        mm = pe.matmul(bank(r % 4), wq[:, c, P * (j % 4):P * (j % 4 + 1)], xT[:, c, :],
                                       start=(c == 0), stop=(c == KC - 1))
                    mm.then_inc(query_done, 1)
                    if j % 4 == 3:
                        pe.wait_ge(query_done, 8 * g + j + 1)
                        pe.nop().then_inc(item_used, 1)
                kT = slot(g, 12)
                pe.wait_ge(query_copied, 8 * (g + 1))
                for t in range(GT):
                    T = GT * g + t
                    if t >= 2:
                        pe.wait_ge(routed, T - 1)
                    for j in range(8):
                        mm = pe.matmul(bank(4 + 2 * (t % 2) + j // 4)[:, P * (j % 4):P * (j % 4 + 1)],
                                       qp_T[:, j, P * t:P * (t + 1)], kT[:, P * j:P * (j + 1)], start=True, stop=True,
                                       skip_group_check=True)
                    mm.then_inc(scores_done, 1)
                pe.wait_ge(scores_done, GT * (g + 1))
                pe.nop().then_inc(item_used, 1)

        @block.scalar
        def _(act):
            chain = [0]

            def after(ins):
                chain[0] += 1
                ins.then_inc(act_chain, 1)
                act.wait_ge(act_chain, chain[0])

            nc.scalar.preload_act_table_set("natural_log_exp_and_others")
            act.wait_ge(const_landed, 16)
            act.wait_ge(zeros_set, 2)

            def expert_steps(g, steps):
                for st in steps:
                    t, e = (st % (GT * NEXP)) // NEXP, st % NEXP
                    T = GT * g + t
                    if e != NEXP - 1:
                        continue
                    if st < GT * NEXP:
                        act.wait_ge(gelu_in, T + 1)
                        nc.scalar.activation(gel[:, :], gel[:, :], ACT.Exp).then_inc(gelu_exp, 1)
                    else:
                        act.wait_ge(var2_ready, T + 1)
                        after(nc.scalar.activation(mv2[:, 3:4], mv2[:, 2:3], ACT.Ln))
                        nc.scalar.activation(mv2[:, 4:5], mv2[:, 3:4], ACT.Exp, scale=-0.5).then_inc(rstd2, 1)
                        act.wait_ge(y_ready, T + 1)
                        dst = (x_mid if T < TILES else out)[(T % TILES) * P:(T % TILES + 1) * P, :]
                        act.dma_start(dst, y[:, :]).then_inc(y_stored, 16)

            for g in range(NG):
                half = g % 2
                share = shares(g)

                def experts(kind, n):
                    if g > 0:
                        expert_steps(g - 1, share[(kind, n)])

                for t in range(GT):
                    for hf in range(2):
                        j = 2 * (GT * g + t) + hf
                        act.wait_ge(x_turned, j + 1)
                        if g > 0:
                            act.wait_ge(query_done, 8 * g)
                        nc.scalar.copy(xT[:, 4 * hf:4 * hf + 4, P * t:P * (t + 1)],
                                       bank(j % 4).rearrange("p (c n) -> p c n", c=4)).then_inc(xT_copied, 1)
                g0 = GW * half
                for j in range(6):
                    act.wait_ge(proj_done, 6 * g + j + 1)
                    src = bank(j % 4)
                    if j == 0:
                        ins = nc.scalar.mul(q_sb[:, :], src, HD ** -0.5)
                    elif j == 1:
                        ins = nc.scalar.copy(k_sb[:, g0:g0 + GW], src)
                    elif j in (2, 3):
                        ins = nc.scalar.mul((q_nsa, q_moba)[j - 2][:, :], src, cst[:, C_QS + j - 2:C_QS + j - 1])
                    else:
                        for r in range(NH):
                            dst = slice(HD * r, HD * (r + 1))
                            if j == 5:
                                ins = nc.scalar.copy(k_moba[dst, g0:g0 + GW], src[0:HD, :])
                                continue
                            nc.scalar.copy(k_slc[dst, g0:g0 + GW], src[64:96, :])
                            nc.scalar.copy(k_win[dst, g0:g0 + GW], src[96:128, :])
                            lost = r if half == 0 else 0
                            nc.scalar.copy(ck_sh[dst, g0 + lost - r:g0 + GW - r], src[0:32, lost:])
                            ins = nc.scalar.copy(cv_sh[dst, g0 + lost - r:g0 + GW - r], src[32:64, lost:])
                    ins.then_inc(proj_copied, 1)
                    experts("proj", j)
                for t in range(GT):
                    act.wait_ge(v_done, GT * g + t + 1)
                    nc.scalar.copy(vals[:, GT * half + t, :], bank(4 + t % 2)[:, 0:236]).then_inc(v_copied, 1)
                act.wait_ge(v_copied, GT * (g + 1))
                nc.scalar.activation(gate_e[:, :, :], vals[:, GT * half:GT * half + GT, 224:236], ACT.Exp,
                                     scale=-1.0).then_inc(gate_exp, 1)
                nc_ = 31 if half == 0 else NCMP
                act.wait_ge(cmp_done, 2 * g + 1)
                for r in range(NH):
                    ins = nc.scalar.copy(kc_T[HD * r:HD * (r + 1), r, 0:nc_], bank(6)[0:HD, 0:nc_])
                ins.then_inc(cmp_copied, 1)
                act.wait_ge(cmp_done, 2 * g + 2)
                nc.scalar.copy(vc[0:nc_, :], bank(7)[0:nc_, 0:HD]).then_inc(cmp_copied, 1)

                for t in range(GT):
                    T = GT * g + t
                    i = T % TILES
                    nct = 8 * i + 7
                    act.wait_ge(zc_scored, T + 1)
                    if T >= 2:
                        act.wait_ge(o_rows_v, T - 1)
                    for h in range(NH):
                        ins = nc.scalar.activation(zc[:, h, 0:nct], zc[:, h, 0:nct], ACT.Exp, scale=-1.0,
                                                   bias=negm_c[:, h:h + 1], accum_out=den[:, T % 2, h:h + 1])
                    ins.then_inc(zc_exp, 1)
                    act.wait_ge(pc_turned, T + 1)
                    nc.scalar.copy(pc_T[0:nct, 0:512], bank(5)[0:nct, :]).then_inc(pc_copied, 1)

                    def p_copy(n):
                        N = 12 * T + n
                        act.wait_ge(p_turned, N + 1)
                        if N >= 2:
                            act.wait_ge(pv_done, N - 1)
                        _, nb = blocks(n, i)
                        w = min(nb, 4) * P
                        ins = nc.scalar.copy(pT_sb[N % 2][:, 0:w], bank(4)[:, 0:w])
                        if nb > 4:
                            ins = nc.scalar.copy(pT_sb[N % 2][:, 512:nb * P], bank(5)[:, 0:nb * P - 512])
                        ins.then_inc(p_copied, 1)

                    for h in range(NH):
                        r = slice(HD * h, HD * (h + 1))
                        ins = nc.scalar.copy(q_heads[r, h, :], q_sb[r, P * t:P * (t + 1)])
                    ins.then_inc(q_spread, 1)
                    for n in range(12):
                        N = 12 * T + n
                        _, nb = blocks(n, i)
                        act.wait_ge(scored, N + 1)
                        dcol = (8, 12, 4)[n // NH] + n % NH
                        z = zb[N % 2][:, 0:nb * P]
                        nc.scalar.activation(z, z, ACT.Exp, scale=-1.0, bias=negm[:, N % 4:N % 4 + 1],
                                             accum_out=den[:, T % 2, dcol:dcol + 1]).then_inc(probs, 1)
                        if n >= 1:
                            p_copy(n - 1)
                        experts("soft", 12 * t + n)
                    p_copy(11)

                    def soft_log(m):
                        M = sb_before(T) + m
                        act.wait_ge(zsb_done, M + 1)
                        if M >= 2:
                            act.wait_ge(sp_ready, M - 1)
                        b = lbuf[M % 2]
                        after(nc.scalar.activation(b, bank(M % 4), ACT.Abs))
                        after(nc.scalar.activation(b, b, ACT.Exp, scale=-1.0))
                        nc.scalar.activation(b, b, ACT.Ln, bias=1.0).then_inc(softplus, 1)

                    soft_log(0)
                    for m in range(i + 1):
                        M = sb_before(T) + m
                        if m + 1 <= i:
                            soft_log(m + 1)
                        act.wait_ge(sb_summed, M + 1)
                        if M >= 2:
                            act.wait_ge(sb_pv, M - 1)
                        nc.scalar.activation(wb[M % 2], bank(M % 4), ACT.Exp).then_inc(sb_w, 1)
                        experts("sb", (t, m))
                    act.wait_ge(sb_pv, sb_before(T) + i + 1)
                    if T >= 1:
                        act.wait_ge(o_turned, T)
                    if t == 0 and g > 0:
                        act.wait_ge(idx_ready, GT * g)
                    nc.scalar.copy(o_row[:, 0:P], bank(5)[:, 0:P]).then_inc(o_rows_a, 1)
                    act.wait_ge(o_turned, T + 1)
                    for b in range(3):
                        ins = nc.scalar.copy((q_sb, q_nsa, q_moba)[b][:, P * t:P * (t + 1)], bank(4)[:, P * b:P * (b + 1)])
                    ins.then_inc(oT_copied, 1)

                def gate_exp_of(k):
                    act.wait_ge(gate_arg, k + 1)
                    nc.scalar.activation(gate_buf[k % 4], gate_buf[k % 4], ACT.Exp).then_inc(gate_sig, 1)

                for k6 in range(24):
                    k = 24 * g + k6
                    act.wait_ge(merge_done, k + 1)
                    eb = gate_buf[k % 4]
                    after(nc.scalar.activation(eb, bank(k % 4), ACT.Abs))
                    after(nc.scalar.activation(eb, eb, ACT.Exp, scale=-1.0))
                    nc.scalar.activation(eb, eb, ACT.Ln, bias=1.0).then_inc(gate_e_done, 1)
                    if k6 >= 1:
                        gate_exp_of(k - 1)
                    experts("merge", k6)
                gate_exp_of(24 * g + 23)
                act.wait_ge(merge_done, 24 * (g + 1))
                for r in range(8):
                    act.wait_ge(mix_turned, 8 * g + r + 1)
                    t, hf = r // 2, r % 2
                    nc.scalar.copy(xT[:, 4 * hf:4 * hf + 4, P * t:P * (t + 1)],
                                   bank(r % 4).rearrange("p (c n) -> p c n", c=4)).then_inc(mixT_copied, 1)
                for t in range(GT):
                    T = GT * g + t
                    experts("ln1", t)
                    act.wait_ge(var_ready, T + 1)
                    after(nc.scalar.activation(mv[:, 3:4], mv[:, 2:3], ACT.Ln))
                    nc.scalar.activation(mv[:, 4:5], mv[:, 3:4], ACT.Exp, scale=-0.5).then_inc(rstd, 1)
                for r in range(8):
                    act.wait_ge(x1_turned, 8 * g + r + 1)
                    t, hf = r // 2, r % 2
                    nc.scalar.copy(xT[:, 4 * hf:4 * hf + 4, P * t:P * (t + 1)],
                                   bank(r % 4).rearrange("p (c n) -> p c n", c=4)).then_inc(x1T_copied, 1)
                for j in range(8):
                    act.wait_ge(query_done, 8 * g + j + 1)
                    nc.scalar.copy(qp_T[:, j, :], bank(j % 4)).then_inc(query_copied, 1)
                    experts("query", j)
                for t in range(GT):
                    T = GT * g + t
                    act.wait_ge(topk_ready, T + 1)
                    nc.scalar.activation(top[:, :, :], top[:, :, :], ACT.Exp).then_inc(top_exp, 1)
                    experts("route", t)
            expert_steps(NG - 1, range(STEPS))
            act.wait_ge(y_stored, 16 * NG * GT)

        @block.vector
        def _(dve):
            v = nc.vector
            chain = [0]

            def after(ins):
                chain[0] += 1
                ins.then_inc(dve_chain, 1)
                dve.wait_ge(dve_chain, chain[0])

            dve.wait_ge(const_landed, 16)
            v.memset(kc_T[:, :, :], 0.0).then_inc(zeros_set, 1)
            v.memset(q_heads[:, :, :], 0.0).then_inc(zeros_set, 1)
            v.memset(pg[:, 0:1], 0.0)
            after(v.memset(pg[:, NCMP + 1:66], 0.0))

            def layer_norm(row, st, m_, ready, done, n, gb):
                for h in range(2):
                    ins = v.bn_stats(st[:, h, :], row[:, 512 * h:512 * (h + 1)])
                after(ins)
                after(v.bn_aggr(m_[:, 0:2], st[:, :, :]))
                v.tensor_scalar(m_[:, 2:3], m_[:, 1:2], LN_EPS, None, ALU.add).then_inc(ready, 1)
                dve.wait_ge(done, n)
                after(v.scalar_tensor_tensor(out=m_[:, 5:6], in0=m_[:, 4:5], scalar=m_[:, 4:5], in1=m_[:, 2:3],
                                             op0=ALU.mult, op1=ALU.mult))
                after(v.tensor_scalar(m_[:, 5:6], m_[:, 5:6], -0.5, 1.5, ALU.mult, ALU.add))
                after(v.tensor_tensor(m_[:, 6:7], m_[:, 5:6], m_[:, 4:5], ALU.mult))
                after(v.tensor_scalar(row, row, m_[:, 0:1], m_[:, 6:7], ALU.subtract, ALU.mult))
                after(v.tensor_tensor(row, row, gb[:, 0, :], ALU.mult))
                return v.tensor_tensor(row, row, gb[:, 1, :], ALU.add)

            def gelu_finish(g, t):
                T = GT * g + t
                dve.wait_ge(gelu_exp, T + 1)
                after(v.tensor_scalar(gel[:, :], gel[:, :], 1.0, None, ALU.add))
                after(v.reciprocal(gel[:, :], gel[:, :]))
                after(v.tensor_tensor(wts[:, t, :], dots[:, t, :], gel[:, :], ALU.mult))
                after(v.tensor_tensor(wts[:, t, :], wts[:, t, :], gw[:, GT * (g % 2) + t, :], ALU.mult))

            def expert_steps(g, steps):
                for st in steps:
                    n = STEPS * g + st
                    t, e = (st % (GT * NEXP)) // NEXP, st % NEXP
                    T = GT * g + t
                    row = rows[:, n % GATHER_SLOTS, :]
                    if st == GT * NEXP:
                        gelu_finish(g, GT - 1)
                    if st >= GT * NEXP and e == 0:
                        if T > 0:
                            dve.wait_ge(y_stored, 16 * T)
                        after(v.tensor_scalar(y[:, :], x1[:, t, :], ALPHA, None, ALU.mult))
                    dve.wait_ge(expert_landed[n % GATHER_SLOTS], 16 * (n // GATHER_SLOTS + 1))
                    if st < GT * NEXP:
                        v.tensor_tensor_reduce(row, row, x1[:, t, :], 1.0, 0.0, ALU.mult, ALU.add,
                                               dots[:, t, e:e + 1]).then_inc(row_used, 1)
                        if e == 3 and t > 0:
                            gelu_finish(g, t - 1)
                        if e == NEXP - 1:
                            dve.wait_ge(row_used, n + 1)
                            dt_ = dots[:, t, :]
                            c1 = -2.0 * (2.0 / 3.141592653589793) ** 0.5
                            after(v.tensor_tensor(gel[:, :], dt_, dt_, ALU.mult))
                            after(v.tensor_scalar(gel[:, :], gel[:, :], 0.044715 * c1, c1, ALU.mult, ALU.add))
                            v.tensor_tensor(gel[:, :], gel[:, :], dt_, ALU.mult).then_inc(gelu_in, 1)
                    else:
                        if e > 0:
                            dve.wait_ge(row_used, n)
                        v.scalar_tensor_tensor(out=y[:, :], in0=row, scalar=wts[:, t, e:e + 1], in1=y[:, :],
                                               op0=ALU.mult, op1=ALU.add).then_inc(row_used, 1)
                        if e == NEXP - 1:
                            dve.wait_ge(row_used, n + 1)
                            dve.wait_ge(ln2_landed, 16 * (g // 2 + 1))
                            layer_norm(y[:, :], stats2, mv2, var2_ready, rstd2, T + 1, ln2_gb).then_inc(y_ready, 1)

            def select_blocks(T):
                i = T % TILES
                nct = 8 * i + 7
                dve.wait_ge(zc_exp, T + 1)
                after(v.tensor_scalar(rden[:, 0:NH], den[:, T % 2, 0:NH], 1e-30, None, ALU.max))
                after(v.reciprocal(rden[:, 0:NH], rden[:, 0:NH]))
                if nct < NCMP:
                    after(v.memset(pg[:, nct + 1:NCMP + 1], 0.0))
                p = pg[:, 1:nct + 1]
                after(v.tensor_scalar(p, zc[:, 0, 0:nct], rden[:, 0:1], None, ALU.mult))
                for h in range(1, NH):
                    after(v.scalar_tensor_tensor(out=p, in0=zc[:, h, 0:nct], scalar=rden[:, h:h + 1], in1=p,
                                                 op0=ALU.mult, op1=ALU.add))
                a, b = imp[:, 0, :], imp[:, 1, :]

                def tap(o):
                    return pg[:, o:o + 4 * (NSEL - 1) + 1:4]

                after(v.tensor_tensor(a, tap(1), tap(2), ALU.add))
                after(v.tensor_tensor(a, a, tap(3), ALU.add))
                after(v.scalar_tensor_tensor(out=a, in0=a, scalar=2.0, in1=tap(0), op0=ALU.mult, op1=ALU.add))
                after(v.tensor_tensor(a, a, tap(4), ALU.add))
                after(v.tensor_tensor(a, a, cst[:, C_F + 14 - 2 * i:C_F + 30 - 2 * i], ALU.add))
                after(v.memset(a[:, 0:1], BIG))
                after(v.max(top8[:, :], a))
                after(v.match_replace(b, top8[:, :], a, 3.0 * BIG))
                after(v.tensor_scalar(b, b, 2.0 * BIG, BIG, ALU.is_lt, ALU.mult))
                w = (i + 1) * P
                nb = w // 64
                after(v.tensor_tensor(selT[:, 0:w].rearrange("p (b n) -> p b n", b=nb),
                                      cst[:, C_T + 1024 - w:C_T + 1024].rearrange("p (b n) -> p b n", b=nb),
                                      b[:, 0:nb].unsqueeze(2).to_broadcast([P, nb, 64]), ALU.add))

            def route(T):
                t = T % GT
                g = T // GT
                sl = GT * (g % 2) + t
                dve.wait_ge(scores_done, T + 1)
                for h in range(PH):
                    for b in range(2):
                        j = 2 * h + b
                        sc = bank(4 + 2 * (t % 2) + j // 4)[:, P * (j % 4):P * (j % 4 + 1)]
                        after(v.max(v8[:, b, :], sc))
                        ins = v.max_index(i8[:, b, :], v8[:, b, :], sc)
                        if j == 7:
                            ins.then_inc(routed, 1)
                            dve.wait_ge(routed, T + 1)
                        else:
                            after(ins)
                    after(v.tensor_copy(i8f[:, :, :], i8[:, :, :]))
                    c3 = cand[:, :].rearrange("p (a b) -> p a b", a=8)
                    v.tensor_tensor(c3, v8[:, 0, :].unsqueeze(2).to_broadcast([P, 8, 8]),
                                    v8[:, 1, :].unsqueeze(1).to_broadcast([P, 8, 8]), ALU.add)
                    after(v.scalar_tensor_tensor(out=cidx[:, :].rearrange("p (a b) -> p a b", a=8),
                                                 in0=i8f[:, 0, :].unsqueeze(2).to_broadcast([P, 8, 8]), scalar=float(NKEYS),
                                                 in1=i8f[:, 1, :].unsqueeze(1).to_broadcast([P, 8, 8]),
                                                 op0=ALU.mult, op1=ALU.add))
                    after(v.max(top[:, h, :], cand[:, :]))
                    after(v.max_index(pos[:, :], top[:, h, :], cand[:, :]))
                    after(v.tensor_copy(posf[:, :], pos[:, :]))
                    e3 = eqbuf.rearrange("p (k n) -> p k n", k=8)
                    after(v.tensor_tensor(e3, posf[:, :].unsqueeze(2).to_broadcast([P, 8, 64]),
                                          cst[:, C_IOTA:C_IOTA + 64].unsqueeze(1).to_broadcast([P, 8, 64]), ALU.is_equal))
                    after(v.tensor_tensor(e3, e3, cidx[:, :].unsqueeze(1).to_broadcast([P, 8, 64]), ALU.mult))
                    after(v.tensor_reduce(idxf[:, 8 * h:8 * h + 8], e3, AX_X, ALU.add))
                v.tensor_scalar(idx[:, sl, :], idxf[:, :], float(N_EXPERTS * (g // 2)), None, ALU.add).then_inc(idx_ready, 1)
                after(v.tensor_copy(topsum[:, :], top[:, :, 0:1].rearrange("p a b -> p (a b)")))
                v.tensor_tensor(top[:, :, :], top[:, :, :], topsum[:, :].unsqueeze(2).to_broadcast([P, PH, TOPK]),
                                ALU.subtract).then_inc(topk_ready, 1)
                dve.wait_ge(top_exp, T + 1)
                after(v.tensor_reduce(topsum[:, :], top[:, :, :], AX_X, ALU.add))
                after(v.reciprocal(topsum[:, :], topsum[:, :]))
                after(v.tensor_tensor(gw[:, sl, :].rearrange("p (h k) -> p h k", h=PH), top[:, :, :],
                                      topsum[:, :].unsqueeze(2).to_broadcast([P, PH, TOPK]), ALU.mult))

            for g in range(NG):
                share = shares(g)

                def experts(kind, n):
                    if g > 0:
                        expert_steps(g - 1, share[(kind, n)])

                for j in range(6):
                    experts("proj", j)
                dve.wait_ge(gate_exp, g + 1)
                after(v.tensor_scalar(gates[:, :, :], gate_e[:, :, :], 1.0, None, ALU.add))
                v.reciprocal(gates[:, :, :], gates[:, :, :]).then_inc(gates_ready, 1)
                for t in range(GT):
                    T = GT * g + t
                    i = T % TILES
                    nct = 8 * i + 7
                    dve.wait_ge(zc_done, T + 1)
                    if T >= 1:
                        dve.wait_ge(pc_turned, T)
                    for h in range(NH):
                        ins = v.tensor_tensor_reduce(zc[:, h, 0:nct], bank(4)[:, nct * h:nct * (h + 1)],
                                                     cst[:, C_C + 56 - 8 * i:C_C + 63], NSA_SLOPES[h], 1e20,
                                                     ALU.add, ALU.min, negm_c[:, h:h + 1])
                    ins.then_inc(zc_scored, 1)
                    for n in range(12):
                        N = 12 * T + n
                        _, nb = blocks(n, i)
                        w = nb * P
                        h = n % NH
                        dve.wait_ge(z_done, N + 1)
                        if N >= 2:
                            dve.wait_ge(p_turned, N - 1)
                        if n < 4:
                            table = cst[:, C_W + 640 - w:C_W + 640]
                        elif n < 8 or i < 4:
                            table = cst[:, C_T + 1024 - w:C_T + 1024]
                        else:
                            table = selT[:, 0:w]
                        slope = (MOBA_SLOPES if n // NH == 1 else NSA_SLOPES)[h]
                        v.tensor_tensor_reduce(zb[N % 2][:, 0:w], pair(2 * (N % 2))[:, 0:w], table, slope, 1e20,
                                               ALU.add, ALU.min, negm[:, N % 4:N % 4 + 1]).then_inc(scored, 1)
                        if n == 3 and i >= 4:
                            dve.wait_ge(pv_done, 12 * T + 1)
                            select_blocks(T)
                        experts("soft", 12 * t + n)
                    for m in range(i + 1):
                        M = sb_before(T) + m
                        dve.wait_ge(softplus, M + 1)
                        if M >= 2:
                            dve.wait_ge(sb_summed, M if m == 2 else M - 1)
                        sp_ = v.scalar_tensor_tensor(out=spb[M % 2], in0=bank(M % 4), scalar=0.0, in1=lbuf[M % 2],
                                                     op0=ALU.max, op1=ALU.add)
                        if m == 0:
                            after(sp_)
                            s3 = spb[M % 2].rearrange("p (h q) -> p h q", h=NH)
                            sp_ = v.tensor_tensor(s3, s3, cst[:, C_PAST:C_PAST + P].unsqueeze(1).to_broadcast([P, NH, P]), ALU.mult)
                        sp_.then_inc(sp_ready, 1)
                        dve.wait_ge(sp_ready, M + 1)
                        if m == 0 or m == i:
                            v.memset(pg[:, 0:1], 0.0).then_inc(acc_ready, 1)
                        else:
                            prev = spb[(M - 1) % 2] if m == 1 else accb[M % 2]
                            if M >= 1:
                                dve.wait_ge(sb_summed, M)
                            v.tensor_tensor(accb[(M + 1) % 2], prev, spb[M % 2], ALU.add).then_inc(acc_ready, 1)
                            dve.wait_ge(acc_ready, M + 1)
                        experts("sb", (t, m))
                    dve.wait_ge(pv_done, 12 * (T + 1))
                    dve.wait_ge(probs, 12 * (T + 1))
                    if T >= 1:
                        dve.wait_ge(o_turned, T)
                    dve.wait_ge(gates_ready, g + 1)
                    after(v.tensor_scalar(rden[:, :], den[:, T % 2, :], 1e-30, None, ALU.max))
                    after(v.reciprocal(rden[:, :], rden[:, :]))
                    after(v.tensor_tensor(rden[:, 0:12].rearrange("p (c h) -> p c h", c=3),
                                          rden[:, 0:12].rearrange("p (c h) -> p c h", c=3),
                                          gates[:, t, :].rearrange("p (h c) -> p c h", c=3), ALU.mult))
                    ob = bank(6 + T % 2)

                    def scaled(dst, col, c):
                        return v.tensor_tensor(dst.rearrange("p (h d) -> p h d", h=NH),
                                               ob[:, col:col + P].rearrange("p (h d) -> p h d", h=NH),
                                               rden[:, 4 * c:4 * c + 4].unsqueeze(2).to_broadcast([P, NH, HD]), ALU.mult)

                    tmp = zc[:, :, :].rearrange("p a b -> p (a b)")
                    o_nsa = o_row[:, P:2 * P]
                    scaled(o_nsa, 0, 0)
                    after(scaled(tmp[:, 0:P], 384, 1))
                    after(v.tensor_tensor(o_nsa, o_nsa, tmp[:, 0:P], ALU.add))
                    after(scaled(tmp[:, 0:P], 128, 2))
                    after(v.tensor_tensor(o_nsa, o_nsa, tmp[:, 0:P], ALU.add))
                    scaled(o_row[:, 2 * P:3 * P], 256, 3).then_inc(o_rows_v, 1)
                def merge_in(k6):
                    k = 24 * g + k6
                    b, hf, t = (k6 // 4) % 3, k6 // 12, k6 % 4
                    dve.wait_ge(gate_sig, k + 1)
                    dst = mix[:, t, 512 * hf:512 * (hf + 1)]
                    eb = gate_buf[k % 4]
                    ins = v.tensor_tensor(dst if b == 0 else eb, bank(4 + k % 4), eb, ALU.mult)
                    if b > 0:
                        after(ins)
                        ins = v.tensor_tensor(dst, dst, eb, ALU.add)
                    ins.then_inc(merged, 1)

                for k6 in range(24):
                    k = 24 * g + k6
                    dve.wait_ge(gate_e_done, k + 1)
                    v.scalar_tensor_tensor(out=gate_buf[k % 4], in0=bank(k % 4), scalar=0.0, in1=gate_buf[k % 4],
                                           op0=ALU.min, op1=ALU.subtract).then_inc(gate_arg, 1)
                    if k6 >= 1:
                        merge_in(k6 - 1)
                    experts("merge", k6)
                merge_in(23)
                dve.wait_ge(ln1_landed, 16 * (g // 2 + 1))
                for t in range(GT):
                    T = GT * g + t
                    m = 2 * GT * g + GT + t
                    experts("ln1", t)
                    dve.wait_ge(row_landed[m % 2], 16 * (m // 2 + 1))
                    for h in range(2):
                        dve.wait_ge(out_done, 8 * g + 2 * t + h + 1)
                        v.scalar_tensor_tensor(out=x1[:, t, 512 * h:512 * (h + 1)], in0=x_row[:, m % 2, 512 * h:512 * (h + 1)],
                                               scalar=ALPHA, in1=bank((8 + 2 * t + h) % 4), op0=ALU.mult, op1=ALU.add)\
                            .then_inc(out_added, 1)
                    dve.wait_ge(out_added, 8 * g + 2 * t + 2)
                    v.memset(mv[:, 7:8], 0.0).then_inc(resid_used, 1)
                    layer_norm(x1[:, t, :], stats, mv, var_ready, rstd, T + 1, ln1_gb).then_inc(ln1_done, 1)
                for j in range(8):
                    experts("query", j)
                for t in range(GT):
                    route(GT * g + t)
                    experts("route", t)
            expert_steps(NG - 1, range(STEPS))


def kernel(**inputs):
    import numpy as np
    import concourse.bacc as bacc
    from concourse.bass_utils import run_bass_kernel_spmd as run

    a = {k: np.asarray(val) for k, val in inputs.items()}
    L = DEPTH

    def slices(w):
        n = w.shape[2]
        return np.ascontiguousarray(w.reshape(L, KC, P, n).transpose(0, 2, 1, 3)).reshape(L, P, KC * n)

    w = a["w_in"]
    col = lambda lo, hi: w[:, :, lo:hi]
    attn_a = slices(np.concatenate([col(0, 128), col(128, 256), col(384, 512), col(716, 844)], axis=2))
    attn_b = slices(np.concatenate([col(512, 544), col(544, 576), col(576, 608), col(640, 672), col(844, 876),
                                    col(256, 384), col(608, 640), col(672, 704), col(876, 908), col(704, 716)], axis=2))
    cmp_w = np.concatenate([slices(a["nsa_w_ck"]), slices(a["nsa_w_cv"]),
                            slices(a["nsa_pe_k"].reshape(L, D, 1)), slices(a["nsa_pe_v"].reshape(L, D, 1))], axis=2)
    merge = []
    for hf in range(2):
        for b, name in enumerate(("w_br_sb", "w_br_nsa", "w_br_moba")):
            lo = 908 + 1024 * b + 512 * hf
            merge.append(np.concatenate([slices(col(lo, lo + 512)), a[name][:, :, 512 * hf:512 * (hf + 1)]], axis=2))
    halves = lambda m: np.stack([slices(m[:, :, 0:512]), slices(m[:, :, 512:1024])], axis=1)
    kk = np.stack([a["peer_k1"], a["peer_k2"]], axis=2)
    arrays = {
        "consts": constants(),
        "x": a["x"].reshape(SEQ, D),
        "attn_a": attn_a,
        "attn_b": np.concatenate([attn_b, cmp_w], axis=2),
        "merge": np.stack(merge, axis=1),
        "w_out_h": halves(a["w_out"]),
        "ln1": np.concatenate([a["ln1_g"], a["ln1_b"]], axis=1).reshape(L, 2, D),
        "w_query": halves(a["peer_wq"].reshape(L, D, D)),
        "keys_T": np.ascontiguousarray(kk.transpose(0, 4, 1, 2, 3)).reshape(L, P, 8 * NKEYS),
        "table_u": a["peer_u"].reshape(L * N_EXPERTS, D),
        "table_v": a["peer_v"].reshape(L * N_EXPERTS, D),
        "ln2": np.concatenate([a["ln2_g"], a["ln2_b"]], axis=1).reshape(L, 2, D),
    }
    nc = bacc.Bacc("TRN2", target_bir_lowering=False, num_devices=1, dynamic_dma_scratch_size=8192)
    arrays = {k: np.ascontiguousarray(val) for k, val in arrays.items()}
    t = {k: nc.dram_tensor(f"in_{k}", val.shape, F32, kind="ExternalInput").ap() for k, val in arrays.items()}
    o = nc.dram_tensor("out_rows", (SEQ, D), F32, kind="ExternalOutput").ap()
    hybrid_layers(nc, t["consts"], t["x"], t["attn_a"], t["attn_b"], None, None, t["merge"], t["w_out_h"], t["ln1"],
                  t["w_query"], t["keys_T"], t["table_u"], t["table_v"], t["ln2"], o)
    r = run(nc, [{f"in_{k}": val for k, val in arrays.items()}], core_ids=[0])
    return r.results[0]["out_rows"].reshape(1, SEQ, D)
```

```python
from contextlib import ExitStack

import concourse.bass as bass
from concourse import mybir

F32 = mybir.dt.float32
I32 = mybir.dt.int32
U32 = mybir.dt.uint32
ALU = mybir.AluOpType
ACT = mybir.ActivationFunctionType
AX_X = mybir.AxisListType.X

P = 128
D = 1024
KC = D // P
SEQ = 1024
DEPTH = 2
HD = 32
NH = 4
CMP_STRIDE, CMP_LEN = 16, 32
NCMP = SEQ // CMP_STRIDE - 1
NSEL = SEQ // 64
NKEYS, TOPK, PH = 128, 8, 4
NEXP = PH * TOPK
N_EXPERTS = NKEYS * NKEYS
ALPHA = (2.0 * DEPTH) ** 0.25
LN_EPS = 1e-5
BIG = 1e30
NSA_SLOPES = [2.0 ** -(2 * h + 1) for h in range(NH)]
MOBA_SLOPES = [2.0 ** -(2 * h + 2) for h in range(NH)]

GT = 4
GW = GT * P
NG = DEPTH * SEQ // GW
TILES = SEQ // P
GATHER_SLOTS = 6
SECTIONS = [(g, 0, GT) for g in range(NG - 1)] + [(NG - 1, 0, GT // 2), (NG - 1, GT // 2, GT // 2)]
ITEM = 9 * 512

C_ID, C_NTRI, C_NONE, C_NEG, C_PAST = 0, 128, 256, 384, 512
C_T = 640
C_W = C_T + 1024
C_C = C_W + 640
C_F = C_C + 63
C_IOTA = C_F + 30
C_QS = C_IOTA + 64
C_END = C_QS + 2


def constants():
    import numpy as np

    c = np.zeros((P, C_END), np.float32)
    p = np.arange(P)[:, None]
    x = np.arange(P)[None, :]
    c[:, C_ID:C_ID + P] = p == x
    c[:, C_NTRI:C_NTRI + P] = np.where(p >= x, -1.0, 0.0)
    c[:, C_NONE:C_NONE + P] = -1.0
    c[:, C_NEG:C_NEG + P] = np.where(p < x, 0.0, -BIG)
    c[:, C_PAST:C_PAST + P] = p < x
    d = p - (np.arange(1024)[None, :] - 896)
    c[:, C_T:C_T + 1024] = np.where(d >= 0, d, BIG)
    d = p - (np.arange(640)[None, :] - 512)
    c[:, C_W:C_W + 640] = np.where((d >= 0) & (d < 512), d, BIG)
    d = p - CMP_STRIDE * (np.arange(63)[None, :] - 56) - (CMP_LEN - 1)
    c[:, C_C:C_C + 63] = np.where(d >= 0, d, BIG)
    r = np.arange(30)[None, :] - 14
    cur = p // 64
    c[:, C_F:C_F + 30] = np.where(r > cur, -BIG, np.where(r >= cur - 1, BIG, 0.0))
    c[:, C_IOTA:C_IOTA + 64] = np.arange(64)[None, :]
    h = np.arange(P) // HD
    c[:, C_QS] = -(HD ** -0.5) / np.array(NSA_SLOPES)[h]
    c[:, C_QS + 1] = -(HD ** -0.5) / np.array(MOBA_SLOPES)[h]
    return c


def sb_before(T):
    i = T % TILES
    return (T // TILES) * (TILES * (TILES + 1) // 2) + i * (i + 1) // 2


def tiles_before(sec):
    return GT * SECTIONS[sec][0] + SECTIONS[sec][1]


def steps_of(sec):
    return 2 * SECTIONS[sec][2] * NEXP


def item_number(sec, k):
    return 11 * sec + 2 * (SECTIONS[sec][0] + 1) + k - 2


def section_points(sec):
    g, t0, nt = SECTIONS[sec]
    pts = []
    if t0 == 0:
        pts = [("proj", n, 1.5) for n in range(6)]
        for t in range(GT):
            i = (g * GT + t) % TILES
            for n in range(12):
                pts.append(("soft", t * 12 + n, 0.6 * (min(i + 1, 5) if n < 4 else i + 1)))
            for m in range(i + 1):
                pts.append(("sb", (t, m), 4.5))
    pts += [("merge", k, 3.0 if t0 == 0 and nt < GT else 6.5) for k in range(6 * nt)]
    pts += [("ln1", t, 5.0) for t in range(nt)]
    pts += [("query", j, 1.7 * nt) for j in range(8)]
    return pts


def shares(sec):
    if sec == 0:
        return {}
    pts = section_points(sec)
    whole = sum(w for _, _, w in pts)
    nt_prev, t0 = SECTIONS[sec - 1][2], SECTIONS[sec][1]
    out, at, last = {}, 0.0, 0
    for kind, n, w in pts:
        at += w
        to = round(steps_of(sec - 1) * at / whole)
        if kind == "ln1" and t0 == 0:
            to = max(to, nt_prev * NEXP + NEXP * n + 1)
        if kind == "proj":
            to = min(to, NEXP + 3)
        to = max(to, last)
        out[(kind, n)] = range(last, to)
        last = to
    return out


def hybrid_layers(nc, consts, x_in, w_attn_a, w_attn_b, w_merge, w_out, ln1, w_query,
                  keys, tab_u, tab_v, ln2, out):
    x_mid = nc.dram_tensor("x_mid", [SEQ, D], F32, kind="Internal").ap()
    ctx = ExitStack()
    with ctx:
        def sb(name, shape, dt=F32):
            return ctx.enter_context(nc.sbuf_tensor(name, shape, dt))

        def sem(name):
            return ctx.enter_context(nc.semaphore(name))

        cst = sb("cst", [P, C_END])
        xT = sb("xT", [P, KC, GW])
        x_row = sb("x_row", [P, 2, D])
        x1 = sb("x1", [P, GT, D])
        y = sb("y", [P, D])
        rows = sb("rows", [P, GATHER_SLOTS, D])
        wring = sb("wring", [P, 2, ITEM])
        q_sb = sb("q_sb", [P, GW])
        q_nsa = sb("q_nsa", [P, GW])
        q_moba = sb("q_moba", [P, GW])
        k_sb = sb("k_sb", [P, SEQ])
        k_slc = sb("k_slc", [P, SEQ])
        k_win = sb("k_win", [P, SEQ])
        k_moba = sb("k_moba", [P, SEQ])
        ck_sh = sb("ck_sh", [P, SEQ])
        cv_sh = sb("cv_sh", [P, SEQ])
        kc_T = sb("kc_T", [P, NH, 64])
        q_heads = sb("q_heads", [P, NH, P])
        vc = sb("vc", [64, HD])
        vals = sb("vals", [P, TILES, 236])
        gate_e = sb("gate_e", [P, GT, 12])
        gates = sb("gates", [P, GT, 12])
        scratch = sb("scratch", [P, 2, 4096])
        ln1_gb = sb("ln1_gb", [P, 2, D])
        ln2_gb = sb("ln2_gb", [P, 2, D])
        row_buf = sb("row_buf", [P, 512])
        zc = sb("zc", [P, NH, 64])
        den = sb("den", [P, 2, 16])
        rden = sb("rden", [P, 16])
        negm = sb("negm", [P, 4])
        negm_c = sb("negm_c", [P, NH])
        pg = sb("pg", [P, 66])
        imp = sb("imp", [P, 3, NSEL])
        top8 = sb("top8", [P, 8])
        stats = sb("stats", [P, 2, 6])
        mv = sb("mv", [P, 8])
        stats2 = sb("stats2", [P, 2, 6])
        mv2 = sb("mv2", [P, 8])
        v8 = sb("v8", [P, 2, 8])
        i8 = sb("i8", [P, 2, 8], U32)
        i8f = sb("i8f", [P, 2, 8])
        cand = sb("cand", [P, 64])
        cidx = sb("cidx", [P, 64])
        pos = sb("pos", [P, 8], U32)
        posf = sb("posf", [P, 8])
        top = sb("top", [P, GT, PH, TOPK])
        topsum = sb("topsum", [P, GT * PH])
        idxf = sb("idxf", [P, NEXP])
        idx = sb("idx", [P, 2 * GT, NEXP], I32)
        gw = sb("gw", [P, 2 * GT, NEXP])
        dots = sb("dots", [P, GT, NEXP])
        gel = sb("gel", [P, NEXP])
        wts = sb("wts", [P, GT, NEXP])

        zb = [scratch[:, 0, 1024 * b:1024 * (b + 1)] for b in range(2)]
        pT_sb = [scratch[:, 0, 2048 + 1024 * b:2048 + 1024 * (b + 1)] for b in range(2)]
        s2 = scratch[:, 1, :]
        lbuf = [s2[:, 512 * b:512 * (b + 1)] for b in range(2)]
        spb = [s2[:, 1024 + 512 * b:1024 + 512 * (b + 1)] for b in range(2)]
        wb = [s2[:, 2048 + 512 * b:2048 + 512 * (b + 1)] for b in range(2)]
        accb = [s2[:, 3072 + 512 * b:3072 + 512 * (b + 1)] for b in range(2)]
        mix = scratch[:, 0, :].rearrange("p (t n) -> p t n", t=GT)
        scores_sb = scratch[:, 0, :].rearrange("p (t n) -> p t n", t=GT)
        qp_T = scratch[:, 1, :].rearrange("p (c n) -> p c n", c=8)
        gate_buf = [s2[:, 512 * b:512 * (b + 1)] for b in range(4)]
        o_row = row_buf[:, 0:384]
        eqbuf = row_buf[:, :]
        selT = s2[:, 2048:3072]
        pc_T = selT

        ps = ctx.enter_context(nc.psum_tensor("ps", [P, 8, 512], F32))

        def bank(b):
            return ps[:, b, :]

        def pair(b):
            return ps[:, b:b + 2, :].rearrange("p a n -> p (a n)")

        ident = cst[:, C_ID:C_ID + P]
        item_landed = [sem("item_landed0"), sem("item_landed1")]
        row_landed = [sem("x_row_landed0"), sem("x_row_landed1")]
        expert_landed = [sem(f"expert_landed{n}") for n in range(GATHER_SLOTS)]
        names = """const_landed ln1_landed ln2_landed item_used x_turned resid_used xT_copied proj_done
            proj_copied v_done v_copied cmp_done cmp_copied gate_exp gates_ready zc_done zc_scored zc_exp
            pc_turned pc_copied z_done scored probs p_turned p_copied pv_done zsb_done softplus sp_ready
            acc_ready sb_summed sb_w sb_pv o_rows_v o_rows_a o_turned oT_copied merge_done gate_e_done
            merged mix_turned mixT_copied out_done out_added var_ready rstd ln1_done x1_turned
            x1T_copied query_done query_copied scores_done topk_ready top_exp scores_copied idx_ready
            row_used gelu_in gelu_exp var2_ready rstd2 y_ready y_stored q_spread zeros_set gate_arg gate_sig dve_chain act_chain""".split()
        s = {n: sem(n) for n in names}

        (const_landed, ln1_landed, ln2_landed, item_used, x_turned, resid_used, xT_copied, proj_done,
         proj_copied, v_done, v_copied, cmp_done, cmp_copied, gate_exp, gates_ready, zc_done, zc_scored,
         zc_exp, pc_turned, pc_copied, z_done, scored, probs, p_turned, p_copied, pv_done, zsb_done,
         softplus, sp_ready, acc_ready, sb_summed, sb_w, sb_pv, o_rows_v, o_rows_a, o_turned, oT_copied,
         merge_done, gate_e_done, merged, mix_turned, mixT_copied, out_done, out_added, var_ready, rstd,
         ln1_done, x1_turned, x1T_copied, query_done, query_copied, scores_done, topk_ready, top_exp,
         scores_copied, idx_ready, row_used, gelu_in, gelu_exp, var2_ready, rstd2, y_ready, y_stored,
         q_spread, zeros_set, gate_arg, gate_sig, dve_chain, act_chain) = [s[n] for n in names]

        def blocks(n, i):
            nb = min(i + 1, 5) if n < 4 else i + 1
            return i + 1 - nb, nb

        def segment_freed(eng, sec, r):
            nt, T0 = SECTIONS[sec][2], tiles_before(sec)
            a = 2 * nt
            if r < 0:
                eng.wait_ge(merged, 6 * (T0 + nt) + r + 1)
            elif r < a:
                eng.wait_ge(mixT_copied, 2 * T0 + r + 1)
            elif r < 2 * a:
                eng.wait_ge(out_added, 2 * T0 + r - a + 1)
            elif r < 3 * a:
                eng.wait_ge(x1T_copied, 2 * T0 + r - 2 * a + 1)
            else:
                eng.wait_ge(query_copied, 8 * sec + r - 3 * a + 1)

        block = ctx.enter_context(nc.Block())

        @block.sync
        def _(sp):
            for g in range(NG):
                layer, half = g // 2, g % 2
                def item(sec, k):
                    n = item_number(sec, k)
                    if n >= 2:
                        sp.wait_ge(item_used, n - 1)
                    src = ([w_attn_a[layer], w_attn_b[layer]] + [w_merge[layer, c] for c in range(6)]
                           + [w_out[layer, h] for h in range(2)] + [w_query[layer, h] for h in range(2)]
                           + [keys[layer]])[k]
                    sp.dma_start(wring[:, n % 2, 0:src.shape[1]], src).then_inc(item_landed[n % 2], 16)

                def x_rows(t, residual):
                    m = 2 * GT * g + GT * residual + t
                    T = GT * g + t
                    if layer > 0 and not residual:
                        sp.wait_ge(y_stored, 16 * (T - TILES + 1))
                    if m >= 2:
                        if t >= 2:
                            if residual:
                                sp.wait_ge(resid_used, T - 1)
                            else:
                                sp.wait_ge(x_turned, 2 * (T - 1))
                        elif residual:
                            sp.wait_ge(x_turned, 2 * (GT * g + t + 3))
                        else:
                            sp.wait_ge(resid_used, GT * (g - 1) + t + 3)
                    src = (x_in if layer == 0 else x_mid)[(T % TILES) * P:(T % TILES + 1) * P, :]
                    sp.dma_start(x_row[:, m % 2, :], src).then_inc(row_landed[m % 2], 16)

                x_rows(0, 0)
                x_rows(1, 0)
                item(g, 0)
                item(g, 1)
                x_rows(2, 0)
                x_rows(3, 0)
                if half == 0:
                    if g > 0:
                        sp.wait_ge(ln1_done, GT * g)
                    sp.dma_start(ln1_gb[:, :, :], ln1[layer].partition_broadcast(P)).then_inc(ln1_landed, 16)
                if g == 0 or g == NG // DEPTH + 1:
                    if g > 0:
                        sp.wait_ge(y_ready, TILES)
                    sp.dma_start(ln2_gb[:, :, :], ln2[layer].partition_broadcast(P)).then_inc(ln2_landed, 16)
                for sec, (sg, t0, nt) in enumerate(SECTIONS):
                    if sg != g:
                        continue
                    for k in range(2, 9):
                        item(sec, k)
                    x_rows(t0, 1)
                    x_rows(t0 + 1, 1)
                    item(sec, 9)
                    for t in range(t0 + 2, t0 + nt):
                        x_rows(t, 1)
                    for k in range(10, 13):
                        item(sec, k)

        @block.gpsimd
        def _(pool):
            for sec, (g, t0, nt) in enumerate(SECTIONS):
                for st in range(steps_of(sec)):
                    n = 2 * NEXP * tiles_before(sec) + st
                    t, e = t0 + (st % (nt * NEXP)) // NEXP, st % NEXP
                    first_half = st < nt * NEXP
                    if first_half and e == 0:
                        pool.wait_ge(idx_ready, GT * g + t + 1)
                    if n >= GATHER_SLOTS:
                        pool.wait_ge(row_used, n - GATHER_SLOTS + 1)
                    pool.indirect_dma_start(
                        rows[:, n % GATHER_SLOTS, :], None, tab_u if first_half else tab_v,
                        bass.IndirectOffsetOnAxis(ap=idx[:, GT * (g % 2) + t, e:e + 1], axis=0),
                    ).then_inc(expert_landed[n % GATHER_SLOTS], 16)

        @block.tensor
        def _(pe):
            pe.wait_ge(const_landed, 16)

            def slot(sec, k):
                n = item_number(sec, k)
                pe.wait_ge(item_landed[n % 2], 16 * (n // 2 + 1))
                return wring[:, n % 2, :]

            def turn(dst, src):
                return pe.matmul(dst, src, ident[0:src.shape[0], 0:src.shape[0]], is_transpose=True,
                                 start=True, stop=True)

            def section(sec):
                g, t0, nt = SECTIONS[sec]
                T0 = tiles_before(sec)
                a = 2 * nt
                pe.wait_ge(oT_copied, GT * (g + 1))
                pe.wait_ge(sb_w, sb_before(GT * (g + 1)))
                if t0 > 0:
                    pe.wait_ge(query_copied, 8 * sec)
                    pe.wait_ge(scores_copied, 2 * T0)
                for c6 in range(6):
                    w = slot(sec, 2 + c6)
                    wg = w[:, 0:KC * 512].rearrange("p (c n) -> p c n", c=KC)
                    oT = (q_sb, q_nsa, q_moba)[c6 % 3]
                    for t in range(t0, t0 + nt):
                        k6 = nt * c6 + t - t0
                        k = 6 * T0 + k6
                        if k6 >= 4:
                            pe.wait_ge(merged, k - 3)
                        for c in range(KC):
                            pe.matmul(bank(k % 4), xT[:, c, P * t:P * (t + 1)], wg[:, c, :], start=(c == 0), stop=(c == KC - 1))
                        mm = pe.matmul(bank(4 + k % 4), oT[:, P * t:P * (t + 1)], w[:, KC * 512:], start=True, stop=True)
                        mm.then_inc(merge_done, 1)
                    pe.wait_ge(merge_done, 6 * T0 + nt * (c6 + 1))
                    pe.nop().then_inc(item_used, 1)
                for r in range(a):
                    t = t0 + r // 2
                    segment_freed(pe, sec, r - 4)
                    pe.wait_ge(merged, 6 * T0 + 5 * nt + r // 2 + 1)
                    for c in range(4):
                        kc = 4 * (r % 2) + c
                        mm = turn(bank(r % 4)[:, P * c:P * (c + 1)], mix[:, t, P * kc:P * (kc + 1)])
                    mm.then_inc(mix_turned, 1)
                wo = [slot(sec, 8 + h)[:, 0:KC * 512].rearrange("p (c n) -> p c n", c=KC) for h in range(2)]
                for r in range(a, 2 * a):
                    t, h = t0 + (r - a) // 2, r % 2
                    segment_freed(pe, sec, r - 4)
                    pe.wait_ge(mixT_copied, 2 * (GT * g + t + 1))
                    for c in range(KC):
                        mm = pe.matmul(bank(r % 4), xT[:, c, P * t:P * (t + 1)], wo[h][:, c, :], start=(c == 0), stop=(c == KC - 1))
                    mm.then_inc(out_done, 1)
                pe.wait_ge(out_done, 2 * (T0 + nt))
                pe.nop().then_inc(item_used, 1)
                pe.nop().then_inc(item_used, 1)
                for r in range(2 * a, 3 * a):
                    t = t0 + (r - 2 * a) // 2
                    segment_freed(pe, sec, r - 4)
                    pe.wait_ge(ln1_done, GT * g + t + 1)
                    for c in range(4):
                        kc = 4 * (r % 2) + c
                        mm = turn(bank(r % 4)[:, P * c:P * (c + 1)], x1[:, t, P * kc:P * (kc + 1)])
                    mm.then_inc(x1_turned, 1)
                pe.wait_ge(x1T_copied, 2 * (T0 + nt))
                toks = slice(P * t0, P * (t0 + nt))
                for j in range(8):
                    if j % 4 == 0:
                        wq = slot(sec, 10 + j // 4)[:, 0:KC * 512].rearrange("p (c n) -> p c n", c=KC)
                    segment_freed(pe, sec, 3 * a + j - 4)
                    for c in range(KC):
                        mm = pe.matmul(bank(j % 4)[:, 0:nt * P], wq[:, c, P * (j % 4):P * (j % 4 + 1)], xT[:, c, toks],
                                       start=(c == 0), stop=(c == KC - 1))
                    mm.then_inc(query_done, 1)
                    if j % 4 == 3:
                        pe.wait_ge(query_done, 8 * sec + j + 1)
                        pe.nop().then_inc(item_used, 1)
                kT = slot(sec, 12)
                pe.wait_ge(query_copied, 8 * (sec + 1))
                for t in range(t0, t0 + nt):
                    T = GT * g + t
                    if t >= t0 + 2:
                        pe.wait_ge(scores_copied, 2 * (T - 1))
                    for j in range(8):
                        mm = pe.matmul(bank(4 + 2 * (t % 2) + j // 4)[:, P * (j % 4):P * (j % 4 + 1)],
                                       qp_T[:, j, P * t:P * (t + 1)], kT[:, P * j:P * (j + 1)], start=True, stop=True,
                                       skip_group_check=True)
                    mm.then_inc(scores_done, 1)
                pe.wait_ge(scores_done, T0 + nt)
                pe.nop().then_inc(item_used, 1)

            for g in range(NG):
                layer, half = g // 2, g % 2
                for t in range(GT):
                    T = GT * g + t
                    m = 2 * GT * g + t
                    pe.wait_ge(row_landed[m % 2], 16 * (m // 2 + 1))
                    for hf in range(2):
                        j = 2 * T + hf
                        if j % 8 >= 4:
                            pe.wait_ge(xT_copied, j - 3)
                        elif g > 0:
                            pe.wait_ge(query_copied, 8 * g)
                        for c in range(4):
                            kc = 4 * hf + c
                            mm = turn(bank(j % 4)[:, P * c:P * (c + 1)], x_row[:, m % 2, P * kc:P * (kc + 1)])
                        mm.then_inc(x_turned, 1)
                pe.wait_ge(xT_copied, 8 * (g + 1))
                wa = slot(g, 0)[:, 0:KC * 512].rearrange("p (c n) -> p c n", c=KC)
                for j in range(6):
                    if j == 4:
                        wb_ = slot(g, 1)[:, 0:KC * 396].rearrange("p (c n) -> p c n", c=KC)
                    if j >= 4:
                        pe.wait_ge(proj_copied, 6 * g + j - 3)
                    for c in range(KC):
                        w = wa[:, c, P * j:P * (j + 1)] if j < 4 else wb_[:, c, 0:P] if j == 4 else wb_[:, c, P:P + HD]
                        mm = pe.matmul(bank(j % 4)[0:w.shape[1], :], w, xT[:, c, :], start=(c == 0), stop=(c == KC - 1))
                    mm.then_inc(proj_done, 1)
                    if j == 3:
                        pe.wait_ge(proj_done, 6 * g + 4)
                        pe.nop().then_inc(item_used, 1)
                if g > 0:
                    pe.wait_ge(scores_copied, 2 * GT * g)
                for t in range(GT):
                    if t >= 2:
                        pe.wait_ge(v_copied, GT * g + t - 1)
                    for c in range(KC):
                        mm = pe.matmul(bank(4 + t % 2)[:, 0:236], xT[:, c, P * t:P * (t + 1)], wb_[:, c, 160:396],
                                       start=(c == 0), stop=(c == KC - 1))
                    mm.then_inc(v_done, 1)
                pe.wait_ge(proj_copied, 6 * g + 6)
                nc_ = 31 if half == 0 else NCMP
                extra = wring[:, item_number(g, 1) % 2, KC * 396:]
                wk_c = extra[:, 0:KC * HD].rearrange("p (c n) -> p c n", c=KC)
                wv_c = extra[:, KC * HD:2 * KC * HD].rearrange("p (c n) -> p c n", c=KC)
                pe_k = extra[:, 2 * KC * HD:2 * KC * HD + KC]
                pe_v = extra[:, 2 * KC * HD + KC:2 * KC * HD + 2 * KC]
                last_tok = CMP_STRIDE * (nc_ - 1) + 1
                for c in range(KC):
                    pe.matmul(bank(6)[0:HD, 0:nc_], wk_c[:, c, :], ck_sh[:, 4 * c:4 * c + last_tok:CMP_STRIDE],
                              start=(c == 0), stop=False)
                    mm = pe.matmul(bank(6)[0:HD, 0:nc_], wk_c[:, c, :], pe_k[:, c:c + 1].to_broadcast([P, nc_]),
                                   start=False, stop=(c == KC - 1))
                mm.then_inc(cmp_done, 1)
                for c in range(KC):
                    pe.matmul(bank(7)[0:nc_, 0:HD], cv_sh[:, 4 * c:4 * c + last_tok:CMP_STRIDE], wv_c[:, c, :],
                              start=(c == 0), stop=False)
                    mm = pe.matmul(bank(7)[0:nc_, 0:HD], pe_v[:, c:c + 1].to_broadcast([P, nc_]), wv_c[:, c, :],
                                   start=False, stop=(c == KC - 1))
                mm.then_inc(cmp_done, 1)
                pe.wait_ge(cmp_done, 2 * (g + 1))
                pe.nop().then_inc(item_used, 1)
                pe.wait_ge(v_copied, GT * (g + 1))
                pe.wait_ge(cmp_copied, 2 * (g + 1))
                for t in range(GT):
                    T = GT * g + t
                    i = T % TILES
                    nct = 8 * i + 7
                    tok = slice(P * t, P * (t + 1))
                    obank = bank(6 + T % 2)

                    def z_unit(n):
                        N = 12 * T + n
                        if N >= 2 and n >= 2:
                            pe.wait_ge(scored, N - 1)
                        k0, nb = blocks(n, i)
                        h = n % NH
                        r = slice(HD * h, HD * (h + 1))
                        q, k = ((q_nsa, k_win), (q_moba, k_moba), (q_nsa, k_slc))[n // NH]
                        z = pair(2 * (N % 2))
                        for a in range(0, nb * P, 512):
                            w = min(512, nb * P - a)
                            mm = pe.matmul(z[:, a:a + w], q[r, tok], k[r, k0 * P + a:k0 * P + a + w],
                                           start=True, stop=True, skip_group_check=True)
                        mm.then_inc(z_done, 1)

                    def p_turn(n):
                        N = 12 * T + n
                        pe.wait_ge(probs, N + 1)
                        if N >= 1:
                            pe.wait_ge(p_copied, N)
                        _, nb = blocks(n, i)
                        for b in range(nb):
                            mm = turn(bank(4 + b // 4)[:, P * (b % 4):P * (b % 4 + 1)], zb[N % 2][:, P * b:P * (b + 1)])
                        mm.then_inc(p_turned, 1)

                    def pv(n):
                        N = 12 * T + n
                        pe.wait_ge(p_copied, N + 1)
                        k0, nb = blocks(n, i)
                        h = n % NH
                        col = (128, 256, 384)[n // NH] + HD * h
                        vcol = (160, 192, 128)[n // NH]
                        for b in range(nb):
                            mm = pe.matmul(obank[:, col:col + HD], pT_sb[N % 2][:, P * b:P * (b + 1)],
                                           vals[:, k0 + b, vcol:vcol + HD], start=False, stop=(b == nb - 1),
                                           skip_group_check=True)
                        mm.then_inc(pv_done, 1)

                    if T >= 1 and t >= 1:
                        pe.wait_ge(sb_w, sb_before(T))
                        pe.wait_ge(oT_copied, T)
                    if T >= 2:
                        pe.wait_ge(o_rows_v, T - 1)
                    pe.matmul(bank(4)[:, 0:NH * nct].rearrange("p (h n) -> p h n", h=NH), q_nsa[:, tok],
                              kc_T[:, :, 0:nct], start=True, stop=True).then_inc(zc_done, 1)
                    z_unit(0)
                    z_unit(1)
                    pe.wait_ge(zc_exp, T + 1)
                    for h in range(NH):
                        mm = turn(bank(5)[0:nct, P * h:P * (h + 1)], zc[:, h, 0:nct])
                    mm.then_inc(pc_turned, 1)
                    pe.wait_ge(pc_copied, T + 1)
                    for h in range(NH):
                        mm = pe.matmul(obank[:, HD * h:HD * (h + 1)], pc_T[0:nct, P * h:P * (h + 1)], vc[0:nct, :],
                                       start=(h == 0), stop=True, skip_group_check=True)
                    for n in range(12):
                        if n + 2 < 12:
                            z_unit(n + 2)
                        p_turn(n)
                        if n >= 1:
                            pv(n - 1)
                    pv(11)

                    def z_sb(m):
                        M = sb_before(T) + m
                        if m < 4:
                            pe.wait_ge(scored, 12 * (T + 1))
                        else:
                            pe.wait_ge(sb_w, M - 3)
                        kb = i - m
                        if m == 0:
                            pe.wait_ge(q_spread, T + 1)
                        pe.matmul(bank(M % 4), k_sb[:, P * kb:P * (kb + 1)], q_heads[:, :, :].rearrange("p h n -> p (h n)"),
                                  start=True, stop=True, skip_group_check=True).then_inc(zsb_done, 1)

                    def suffix(m):
                        M = sb_before(T) + m
                        pe.wait_ge(sp_ready, M + 1)
                        if m == 0:
                            pe.matmul(bank(M % 4).rearrange("p (h q) -> p h q", h=NH), ident,
                                      cst[:, C_NEG:C_NEG + P].unsqueeze(1).to_broadcast([P, NH, P]),
                                      start=False, stop=True, skip_group_check=True)
                        if m == 1:
                            pe.matmul(bank(M % 4), cst[:, C_NONE:C_NONE + P], spb[(M - 1) % 2],
                                      start=False, stop=True, skip_group_check=True)
                        if m >= 2:
                            pe.wait_ge(acc_ready, M)
                            pe.matmul(bank(M % 4), cst[:, C_NONE:C_NONE + P], accb[M % 2],
                                      start=False, stop=True, skip_group_check=True)
                        pe.matmul(bank(M % 4), cst[:, C_NTRI:C_NTRI + P], spb[M % 2],
                                  start=False, stop=True, skip_group_check=True).then_inc(sb_summed, 1)

                    def pv_sb(m):
                        M = sb_before(T) + m
                        pe.wait_ge(sb_w, M + 1)
                        if m == 0:
                            pe.wait_ge(p_copied, 12 * (T + 1))
                        for h in range(NH):
                            mm = pe.matmul(bank(5)[:, HD * h:HD * (h + 1)], wb[M % 2][:, P * h:P * (h + 1)],
                                           vals[:, i - m, HD * h:HD * (h + 1)], start=(m == 0 and h == 0), stop=(m == i),
                                           skip_group_check=True)
                        mm.then_inc(sb_pv, 1)

                    for m in range(min(3, i + 1)):
                        z_sb(m)
                    for m in range(i + 1):
                        if m + 3 <= i:
                            z_sb(m + 3)
                        suffix(m)
                        if m >= 1:
                            pv_sb(m - 1)
                    pv_sb(i)
                    pe.wait_ge(o_rows_v, T + 1)
                    pe.wait_ge(o_rows_a, T + 1)
                    for b in range(3):
                        mm = turn(bank(4)[:, P * b:P * (b + 1)], o_row[:, P * b:P * (b + 1)])
                    mm.then_inc(o_turned, 1)

                for sec, (sg, t0, nt) in enumerate(SECTIONS):
                    if sg == g:
                        section(sec)

        @block.scalar
        def _(act):
            chain = [0]

            def after(ins):
                chain[0] += 1
                ins.then_inc(act_chain, 1)
                act.wait_ge(act_chain, chain[0])

            act.dma_start(cst[:, :], consts).then_inc(const_landed, 16)
            nc.scalar.preload_act_table_set("natural_log_exp_and_others")
            act.wait_ge(const_landed, 16)
            act.wait_ge(zeros_set, 2)

            def expert_steps(sec, steps):
                g, t0, nt = SECTIONS[sec]
                for st in steps:
                    t, e = t0 + (st % (nt * NEXP)) // NEXP, st % NEXP
                    T = GT * g + t
                    if e != NEXP - 1:
                        continue
                    if st < nt * NEXP:
                        act.wait_ge(gelu_in, T + 1)
                        nc.scalar.activation(gel[:, :], gel[:, :], ACT.Exp).then_inc(gelu_exp, 1)
                    else:
                        act.wait_ge(var2_ready, T + 1)
                        after(nc.scalar.activation(mv2[:, 3:4], mv2[:, 2:3], ACT.Ln))
                        nc.scalar.activation(mv2[:, 4:5], mv2[:, 3:4], ACT.Exp, scale=-0.5).then_inc(rstd2, 1)
                        act.wait_ge(y_ready, T + 1)
                        dst = (x_mid if T < TILES else out)[(T % TILES) * P:(T % TILES + 1) * P, :]
                        act.dma_start(dst, y[:, :]).then_inc(y_stored, 16)

            def expert_gates(sec):
                _, t0, nt = SECTIONS[sec]
                act.wait_ge(topk_ready, tiles_before(sec) + nt)
                act_top = top[:, t0:t0 + nt, :, :]
                nc.scalar.activation(act_top, act_top, ACT.Exp).then_inc(top_exp, 1)

            def section(sec):
                g, t0, nt = SECTIONS[sec]
                T0 = tiles_before(sec)
                share = shares(sec)

                def experts(kind, n):
                    if sec > 0:
                        expert_steps(sec - 1, share[(kind, n)])

                if t0 > 0:
                    expert_gates(sec - 1)

                def gate_exp_of(k):
                    act.wait_ge(gate_arg, k + 1)
                    nc.scalar.activation(gate_buf[k % 4], gate_buf[k % 4], ACT.Exp).then_inc(gate_sig, 1)

                for k6 in range(6 * nt):
                    k = 6 * T0 + k6
                    act.wait_ge(merge_done, k + 1)
                    eb = gate_buf[k % 4]
                    after(nc.scalar.activation(eb, bank(k % 4), ACT.Abs))
                    after(nc.scalar.activation(eb, eb, ACT.Exp, scale=-1.0))
                    nc.scalar.activation(eb, eb, ACT.Ln, bias=1.0).then_inc(gate_e_done, 1)
                    if k6 >= 1:
                        gate_exp_of(k - 1)
                    experts("merge", k6)
                gate_exp_of(6 * (T0 + nt) - 1)
                act.wait_ge(merge_done, 6 * (T0 + nt))

                def copy_turned(turned, copied):
                    for r in range(2 * nt):
                        act.wait_ge(turned, 2 * T0 + r + 1)
                        t, hf = t0 + r // 2, r % 2
                        nc.scalar.copy(xT[:, 4 * hf:4 * hf + 4, P * t:P * (t + 1)],
                                       bank(r % 4).rearrange("p (c n) -> p c n", c=4)).then_inc(copied, 1)

                copy_turned(mix_turned, mixT_copied)
                for t in range(nt):
                    experts("ln1", t)
                    act.wait_ge(var_ready, T0 + t + 1)
                    after(nc.scalar.activation(mv[:, 3:4], mv[:, 2:3], ACT.Ln))
                    nc.scalar.activation(mv[:, 4:5], mv[:, 3:4], ACT.Exp, scale=-0.5).then_inc(rstd, 1)
                copy_turned(x1_turned, x1T_copied)
                for j in range(8):
                    act.wait_ge(query_done, 8 * sec + j + 1)
                    nc.scalar.copy(qp_T[:, j, P * t0:P * (t0 + nt)], bank(j % 4)[:, 0:nt * P]).then_inc(query_copied, 1)
                    experts("query", j)
                for t in range(t0, t0 + nt):
                    act.wait_ge(scores_done, GT * g + t + 1)
                    for h in range(2):
                        nc.scalar.copy(scores_sb[:, t, 512 * h:512 * (h + 1)], bank(4 + 2 * (t % 2) + h))\
                            .then_inc(scores_copied, 1)

            for g in range(NG):
                half = g % 2
                share = shares(g)

                def experts(kind, n):
                    if g > 0:
                        expert_steps(g - 1, share[(kind, n)])

                for t in range(GT):
                    for hf in range(2):
                        j = 2 * (GT * g + t) + hf
                        act.wait_ge(x_turned, j + 1)
                        if g > 0:
                            act.wait_ge(query_done, 8 * g)
                        nc.scalar.copy(xT[:, 4 * hf:4 * hf + 4, P * t:P * (t + 1)],
                                       bank(j % 4).rearrange("p (c n) -> p c n", c=4)).then_inc(xT_copied, 1)
                g0 = GW * half
                for j in range(6):
                    act.wait_ge(proj_done, 6 * g + j + 1)
                    src = bank(j % 4)
                    if j == 0:
                        ins = nc.scalar.mul(q_sb[:, :], src, HD ** -0.5)
                    elif j == 1:
                        ins = nc.scalar.copy(k_sb[:, g0:g0 + GW], src)
                    elif j in (2, 3):
                        ins = nc.scalar.mul((q_nsa, q_moba)[j - 2][:, :], src, cst[:, C_QS + j - 2:C_QS + j - 1])
                    else:
                        for r in range(NH):
                            dst = slice(HD * r, HD * (r + 1))
                            if j == 5:
                                ins = nc.scalar.copy(k_moba[dst, g0:g0 + GW], src[0:HD, :])
                                continue
                            nc.scalar.copy(k_slc[dst, g0:g0 + GW], src[64:96, :])
                            nc.scalar.copy(k_win[dst, g0:g0 + GW], src[96:128, :])
                            lost = r if half == 0 else 0
                            nc.scalar.copy(ck_sh[dst, g0 + lost - r:g0 + GW - r], src[0:32, lost:])
                            ins = nc.scalar.copy(cv_sh[dst, g0 + lost - r:g0 + GW - r], src[32:64, lost:])
                    ins.then_inc(proj_copied, 1)
                    experts("proj", j)
                for t in range(GT):
                    act.wait_ge(v_done, GT * g + t + 1)
                    nc.scalar.copy(vals[:, GT * half + t, :], bank(4 + t % 2)[:, 0:236]).then_inc(v_copied, 1)
                if g > 0:
                    expert_gates(g - 1)
                act.wait_ge(v_copied, GT * (g + 1))
                nc.scalar.activation(gate_e[:, :, :], vals[:, GT * half:GT * half + GT, 224:236], ACT.Exp,
                                     scale=-1.0).then_inc(gate_exp, 1)
                nc_ = 31 if half == 0 else NCMP
                act.wait_ge(cmp_done, 2 * g + 1)
                for r in range(NH):
                    ins = nc.scalar.copy(kc_T[HD * r:HD * (r + 1), r, 0:nc_], bank(6)[0:HD, 0:nc_])
                ins.then_inc(cmp_copied, 1)
                act.wait_ge(cmp_done, 2 * g + 2)
                nc.scalar.copy(vc[0:nc_, :], bank(7)[0:nc_, 0:HD]).then_inc(cmp_copied, 1)

                for t in range(GT):
                    T = GT * g + t
                    i = T % TILES
                    nct = 8 * i + 7
                    act.wait_ge(zc_scored, T + 1)
                    if T >= 2:
                        act.wait_ge(o_rows_v, T - 1)
                    for h in range(NH):
                        ins = nc.scalar.activation(zc[:, h, 0:nct], zc[:, h, 0:nct], ACT.Exp, scale=-1.0,
                                                   bias=negm_c[:, h:h + 1], accum_out=den[:, T % 2, h:h + 1])
                    ins.then_inc(zc_exp, 1)
                    act.wait_ge(pc_turned, T + 1)
                    nc.scalar.copy(pc_T[0:nct, 0:512], bank(5)[0:nct, :]).then_inc(pc_copied, 1)

                    def p_copy(n):
                        N = 12 * T + n
                        act.wait_ge(p_turned, N + 1)
                        if N >= 2:
                            act.wait_ge(pv_done, N - 1)
                        _, nb = blocks(n, i)
                        w = min(nb, 4) * P
                        ins = nc.scalar.copy(pT_sb[N % 2][:, 0:w], bank(4)[:, 0:w])
                        if nb > 4:
                            ins = nc.scalar.copy(pT_sb[N % 2][:, 512:nb * P], bank(5)[:, 0:nb * P - 512])
                        ins.then_inc(p_copied, 1)

                    for h in range(NH):
                        r = slice(HD * h, HD * (h + 1))
                        ins = nc.scalar.copy(q_heads[r, h, :], q_sb[r, P * t:P * (t + 1)])
                    ins.then_inc(q_spread, 1)
                    for n in range(12):
                        N = 12 * T + n
                        _, nb = blocks(n, i)
                        act.wait_ge(scored, N + 1)
                        dcol = (8, 12, 4)[n // NH] + n % NH
                        z = zb[N % 2][:, 0:nb * P]
                        nc.scalar.activation(z, z, ACT.Exp, scale=-1.0, bias=negm[:, N % 4:N % 4 + 1],
                                             accum_out=den[:, T % 2, dcol:dcol + 1]).then_inc(probs, 1)
                        if n >= 1:
                            p_copy(n - 1)
                        experts("soft", 12 * t + n)
                    p_copy(11)

                    def soft_log(m):
                        M = sb_before(T) + m
                        act.wait_ge(zsb_done, M + 1)
                        if M >= 2:
                            act.wait_ge(sp_ready, M - 1)
                        b = lbuf[M % 2]
                        after(nc.scalar.activation(b, bank(M % 4), ACT.Abs))
                        after(nc.scalar.activation(b, b, ACT.Exp, scale=-1.0))
                        nc.scalar.activation(b, b, ACT.Ln, bias=1.0).then_inc(softplus, 1)

                    for m in range(min(2, i + 1)):
                        soft_log(m)
                    for m in range(i + 1):
                        M = sb_before(T) + m
                        if m + 2 <= i:
                            soft_log(m + 2)
                        act.wait_ge(sb_summed, M + 1)
                        if M >= 2:
                            act.wait_ge(sb_pv, M - 1)
                        nc.scalar.activation(wb[M % 2], bank(M % 4), ACT.Exp).then_inc(sb_w, 1)
                        experts("sb", (t, m))
                    act.wait_ge(sb_pv, sb_before(T) + i + 1)
                    if T >= 1:
                        act.wait_ge(o_turned, T)
                    if t == 0 and g > 0:
                        act.wait_ge(idx_ready, GT * g)
                    nc.scalar.copy(o_row[:, 0:P], bank(5)[:, 0:P]).then_inc(o_rows_a, 1)
                    act.wait_ge(o_turned, T + 1)
                    for b in range(3):
                        ins = nc.scalar.copy((q_sb, q_nsa, q_moba)[b][:, P * t:P * (t + 1)], bank(4)[:, P * b:P * (b + 1)])
                    ins.then_inc(oT_copied, 1)

                for sec, (sg, t0, nt) in enumerate(SECTIONS):
                    if sg == g:
                        section(sec)
            expert_gates(len(SECTIONS) - 1)
            expert_steps(len(SECTIONS) - 1, range(steps_of(len(SECTIONS) - 1)))
            act.wait_ge(y_stored, 16 * NG * GT)

        @block.vector
        def _(dve):
            v = nc.vector
            chain = [0]

            def after(ins):
                chain[0] += 1
                ins.then_inc(dve_chain, 1)
                dve.wait_ge(dve_chain, chain[0])

            dve.wait_ge(const_landed, 16)
            v.memset(kc_T[:, :, :], 0.0).then_inc(zeros_set, 1)
            v.memset(q_heads[:, :, :], 0.0).then_inc(zeros_set, 1)
            v.memset(pg[:, 0:1], 0.0)
            after(v.memset(pg[:, NCMP + 1:66], 0.0))

            def layer_norm(row, st, m_, ready, done, n, gb):
                for h in range(2):
                    ins = v.bn_stats(st[:, h, :], row[:, 512 * h:512 * (h + 1)])
                after(ins)
                after(v.bn_aggr(m_[:, 0:2], st[:, :, :]))
                v.tensor_scalar(m_[:, 2:3], m_[:, 1:2], LN_EPS, None, ALU.add).then_inc(ready, 1)
                dve.wait_ge(done, n)
                after(v.scalar_tensor_tensor(out=m_[:, 5:6], in0=m_[:, 4:5], scalar=m_[:, 4:5], in1=m_[:, 2:3],
                                             op0=ALU.mult, op1=ALU.mult))
                after(v.tensor_scalar(m_[:, 5:6], m_[:, 5:6], -0.5, 1.5, ALU.mult, ALU.add))
                after(v.tensor_tensor(m_[:, 6:7], m_[:, 5:6], m_[:, 4:5], ALU.mult))
                after(v.tensor_scalar(row, row, m_[:, 0:1], m_[:, 6:7], ALU.subtract, ALU.mult))
                after(v.tensor_tensor(row, row, gb[:, 0, :], ALU.mult))
                return v.tensor_tensor(row, row, gb[:, 1, :], ALU.add)

            def gelu_finish(g, t):
                T = GT * g + t
                dve.wait_ge(gelu_exp, T + 1)
                after(v.tensor_scalar(gel[:, :], gel[:, :], 1.0, None, ALU.add))
                after(v.reciprocal(gel[:, :], gel[:, :]))
                after(v.tensor_tensor(wts[:, t, :], dots[:, t, :], gel[:, :], ALU.mult))
                after(v.tensor_tensor(wts[:, t, :], wts[:, t, :], gw[:, GT * (g % 2) + t, :], ALU.mult))

            def expert_steps(sec, steps):
                g, t0, nt = SECTIONS[sec]
                for st in steps:
                    n = 2 * NEXP * tiles_before(sec) + st
                    t, e = t0 + (st % (nt * NEXP)) // NEXP, st % NEXP
                    T = GT * g + t
                    row = rows[:, n % GATHER_SLOTS, :]
                    if st == nt * NEXP:
                        gelu_finish(g, t0 + nt - 1)
                    if st >= nt * NEXP and e == 0:
                        if T > 0:
                            dve.wait_ge(y_stored, 16 * T)
                        after(v.tensor_scalar(y[:, :], x1[:, t, :], ALPHA, None, ALU.mult))
                    dve.wait_ge(expert_landed[n % GATHER_SLOTS], 16 * (n // GATHER_SLOTS + 1))
                    if st < nt * NEXP:
                        v.tensor_tensor_reduce(row, row, x1[:, t, :], 1.0, 0.0, ALU.mult, ALU.add,
                                               dots[:, t, e:e + 1]).then_inc(row_used, 1)
                        if e == 3 and t > t0:
                            gelu_finish(g, t - 1)
                        if e == NEXP - 1:
                            dve.wait_ge(row_used, n + 1)
                            dt_ = dots[:, t, :]
                            c1 = -2.0 * (2.0 / 3.141592653589793) ** 0.5
                            after(v.tensor_tensor(gel[:, :], dt_, dt_, ALU.mult))
                            after(v.tensor_scalar(gel[:, :], gel[:, :], 0.044715 * c1, c1, ALU.mult, ALU.add))
                            v.tensor_tensor(gel[:, :], gel[:, :], dt_, ALU.mult).then_inc(gelu_in, 1)
                    else:
                        if e > 0:
                            dve.wait_ge(row_used, n)
                        v.scalar_tensor_tensor(out=y[:, :], in0=row, scalar=wts[:, t, e:e + 1], in1=y[:, :],
                                               op0=ALU.mult, op1=ALU.add).then_inc(row_used, 1)
                        if e == NEXP - 1:
                            dve.wait_ge(row_used, n + 1)
                            dve.wait_ge(ln2_landed, 16 * (g // 2 + 1))
                            layer_norm(y[:, :], stats2, mv2, var2_ready, rstd2, T + 1, ln2_gb).then_inc(y_ready, 1)

            def select_blocks(T):
                i = T % TILES
                nct = 8 * i + 7
                dve.wait_ge(zc_exp, T + 1)
                after(v.tensor_scalar(rden[:, 0:NH], den[:, T % 2, 0:NH], 1e-30, None, ALU.max))
                after(v.reciprocal(rden[:, 0:NH], rden[:, 0:NH]))
                if nct < NCMP:
                    after(v.memset(pg[:, nct + 1:NCMP + 1], 0.0))
                p = pg[:, 1:nct + 1]
                after(v.tensor_scalar(p, zc[:, 0, 0:nct], rden[:, 0:1], None, ALU.mult))
                for h in range(1, NH):
                    after(v.scalar_tensor_tensor(out=p, in0=zc[:, h, 0:nct], scalar=rden[:, h:h + 1], in1=p,
                                                 op0=ALU.mult, op1=ALU.add))
                a, b = imp[:, 0, :], imp[:, 1, :]

                def tap(o):
                    return pg[:, o:o + 4 * (NSEL - 1) + 1:4]

                after(v.tensor_tensor(a, tap(1), tap(2), ALU.add))
                after(v.tensor_tensor(a, a, tap(3), ALU.add))
                after(v.scalar_tensor_tensor(out=a, in0=a, scalar=2.0, in1=tap(0), op0=ALU.mult, op1=ALU.add))
                after(v.tensor_tensor(a, a, tap(4), ALU.add))
                after(v.tensor_tensor(a, a, cst[:, C_F + 14 - 2 * i:C_F + 30 - 2 * i], ALU.add))
                after(v.memset(a[:, 0:1], BIG))
                after(v.max(top8[:, :], a))
                after(v.match_replace(b, top8[:, :], a, 3.0 * BIG))
                after(v.tensor_scalar(b, b, 2.0 * BIG, BIG, ALU.is_lt, ALU.mult))
                w = (i + 1) * P
                nb = w // 64
                after(v.tensor_tensor(selT[:, 0:w].rearrange("p (b n) -> p b n", b=nb),
                                      cst[:, C_T + 1024 - w:C_T + 1024].rearrange("p (b n) -> p b n", b=nb),
                                      b[:, 0:nb].unsqueeze(2).to_broadcast([P, nb, 64]), ALU.add))

            def route(T):
                t = T % GT
                g = T // GT
                sl = GT * (g % 2) + t
                dve.wait_ge(scores_copied, 2 * (T + 1))
                for h in range(PH):
                    for b in range(2):
                        j = 2 * h + b
                        sc = scores_sb[:, t, P * j:P * (j + 1)]
                        after(v.max(v8[:, b, :], sc))
                        after(v.max_index(i8[:, b, :], v8[:, b, :], sc))
                    after(v.tensor_copy(i8f[:, :, :], i8[:, :, :]))
                    c3 = cand[:, :].rearrange("p (a b) -> p a b", a=8)
                    v.tensor_tensor(c3, v8[:, 0, :].unsqueeze(2).to_broadcast([P, 8, 8]),
                                    v8[:, 1, :].unsqueeze(1).to_broadcast([P, 8, 8]), ALU.add)
                    after(v.scalar_tensor_tensor(out=cidx[:, :].rearrange("p (a b) -> p a b", a=8),
                                                 in0=i8f[:, 0, :].unsqueeze(2).to_broadcast([P, 8, 8]), scalar=float(NKEYS),
                                                 in1=i8f[:, 1, :].unsqueeze(1).to_broadcast([P, 8, 8]),
                                                 op0=ALU.mult, op1=ALU.add))
                    after(v.max(top[:, t, h, :], cand[:, :]))
                    after(v.max_index(pos[:, :], top[:, t, h, :], cand[:, :]))
                    after(v.tensor_copy(posf[:, :], pos[:, :]))
                    e3 = eqbuf.rearrange("p (k n) -> p k n", k=8)
                    after(v.tensor_tensor(e3, posf[:, :].unsqueeze(2).to_broadcast([P, 8, 64]),
                                          cst[:, C_IOTA:C_IOTA + 64].unsqueeze(1).to_broadcast([P, 8, 64]), ALU.is_equal))
                    after(v.tensor_tensor(e3, e3, cidx[:, :].unsqueeze(1).to_broadcast([P, 8, 64]), ALU.mult))
                    after(v.tensor_reduce(idxf[:, 8 * h:8 * h + 8], e3, AX_X, ALU.add))
                v.tensor_scalar(idx[:, sl, :], idxf[:, :], float(N_EXPERTS * (g // 2)), None, ALU.add).then_inc(idx_ready, 1)
                largest = topsum[:, PH * t:PH * (t + 1)]
                after(v.tensor_copy(largest, top[:, t, :, 0:1].rearrange("p a b -> p (a b)")))
                v.tensor_tensor(top[:, t, :, :], top[:, t, :, :], largest.unsqueeze(2).to_broadcast([P, PH, TOPK]),
                                ALU.subtract).then_inc(topk_ready, 1)

            def expert_gates(sec):
                g, t0, nt = SECTIONS[sec]
                dve.wait_ge(top_exp, sec + 1)
                rows_ = top[:, t0:t0 + nt, :, :].rearrange("p t h k -> p (t h) k")
                sums = topsum[:, 0:PH * nt]
                after(v.tensor_reduce(sums, rows_, AX_X, ALU.add))
                after(v.reciprocal(sums, sums))
                n = GT * (g % 2) + t0
                after(v.tensor_tensor(gw[:, n:n + nt, :].rearrange("p t (h k) -> p (t h) k", h=PH), rows_,
                                      sums.unsqueeze(2).to_broadcast([P, nt * PH, TOPK]), ALU.mult))

            def section(sec):
                g, t0, nt = SECTIONS[sec]
                T0 = tiles_before(sec)
                share = shares(sec)

                def experts(kind, n):
                    if sec > 0:
                        expert_steps(sec - 1, share[(kind, n)])

                if t0 > 0:
                    expert_gates(sec - 1)

                def merge_in(k6):
                    k = 6 * T0 + k6
                    b, hf, t = (k6 // nt) % 3, k6 // (3 * nt), t0 + k6 % nt
                    dve.wait_ge(gate_sig, k + 1)
                    dst = mix[:, t, 512 * hf:512 * (hf + 1)]
                    eb = gate_buf[k % 4]
                    ins = v.tensor_tensor(dst if b == 0 else eb, bank(4 + k % 4), eb, ALU.mult)
                    if b > 0:
                        after(ins)
                        ins = v.tensor_tensor(dst, dst, eb, ALU.add)
                    ins.then_inc(merged, 1)

                for k6 in range(6 * nt):
                    k = 6 * T0 + k6
                    dve.wait_ge(gate_e_done, k + 1)
                    v.scalar_tensor_tensor(out=gate_buf[k % 4], in0=bank(k % 4), scalar=0.0, in1=gate_buf[k % 4],
                                           op0=ALU.min, op1=ALU.subtract).then_inc(gate_arg, 1)
                    if k6 >= 1:
                        merge_in(k6 - 1)
                    experts("merge", k6)
                merge_in(6 * nt - 1)
                dve.wait_ge(ln1_landed, 16 * (g // 2 + 1))
                for tt in range(nt):
                    t, T = t0 + tt, T0 + tt
                    m = 2 * GT * g + GT + t
                    experts("ln1", tt)
                    dve.wait_ge(row_landed[m % 2], 16 * (m // 2 + 1))
                    for h in range(2):
                        dve.wait_ge(out_done, 2 * T + h + 1)
                        v.scalar_tensor_tensor(out=x1[:, t, 512 * h:512 * (h + 1)], in0=x_row[:, m % 2, 512 * h:512 * (h + 1)],
                                               scalar=ALPHA, in1=bank((2 * tt + h) % 4), op0=ALU.mult, op1=ALU.add)\
                            .then_inc(out_added, 1)
                    dve.wait_ge(out_added, 2 * T + 2)
                    v.memset(mv[:, 7:8], 0.0).then_inc(resid_used, 1)
                    layer_norm(x1[:, t, :], stats, mv, var_ready, rstd, T + 1, ln1_gb).then_inc(ln1_done, 1)
                for j in range(8):
                    experts("query", j)
                for t in range(t0, t0 + nt):
                    route(GT * g + t)

            for g in range(NG):
                share = shares(g)

                def experts(kind, n):
                    if g > 0:
                        expert_steps(g - 1, share[(kind, n)])

                for j in range(6):
                    experts("proj", j)
                if g > 0:
                    expert_gates(g - 1)
                dve.wait_ge(gate_exp, g + 1)
                after(v.tensor_scalar(gates[:, :, :], gate_e[:, :, :], 1.0, None, ALU.add))
                v.reciprocal(gates[:, :, :], gates[:, :, :]).then_inc(gates_ready, 1)
                for t in range(GT):
                    T = GT * g + t
                    i = T % TILES
                    nct = 8 * i + 7
                    dve.wait_ge(zc_done, T + 1)
                    if T >= 1:
                        dve.wait_ge(pc_turned, T)
                    for h in range(NH):
                        ins = v.tensor_tensor_reduce(zc[:, h, 0:nct], bank(4)[:, nct * h:nct * (h + 1)],
                                                     cst[:, C_C + 56 - 8 * i:C_C + 63], NSA_SLOPES[h], 1e20,
                                                     ALU.add, ALU.min, negm_c[:, h:h + 1])
                    ins.then_inc(zc_scored, 1)
                    for n in range(12):
                        N = 12 * T + n
                        _, nb = blocks(n, i)
                        w = nb * P
                        h = n % NH
                        dve.wait_ge(z_done, N + 1)
                        if N >= 2:
                            dve.wait_ge(p_turned, N - 1)
                        if n < 4:
                            table = cst[:, C_W + 640 - w:C_W + 640]
                        elif n < 8 or i < 4:
                            table = cst[:, C_T + 1024 - w:C_T + 1024]
                        else:
                            table = selT[:, 0:w]
                        slope = (MOBA_SLOPES if n // NH == 1 else NSA_SLOPES)[h]
                        v.tensor_tensor_reduce(zb[N % 2][:, 0:w], pair(2 * (N % 2))[:, 0:w], table, slope, 1e20,
                                               ALU.add, ALU.min, negm[:, N % 4:N % 4 + 1]).then_inc(scored, 1)
                        if n == 3 and i >= 4:
                            dve.wait_ge(pv_done, 12 * T + 1)
                            select_blocks(T)
                        experts("soft", 12 * t + n)
                    for m in range(i + 1):
                        M = sb_before(T) + m
                        dve.wait_ge(softplus, M + 1)
                        if M >= 2:
                            dve.wait_ge(sb_summed, M if m == 2 else M - 1)
                        sp_ = v.scalar_tensor_tensor(out=spb[M % 2], in0=bank(M % 4), scalar=0.0, in1=lbuf[M % 2],
                                                     op0=ALU.max, op1=ALU.add)
                        if m == 0:
                            after(sp_)
                            s3 = spb[M % 2].rearrange("p (h q) -> p h q", h=NH)
                            sp_ = v.tensor_tensor(s3, s3, cst[:, C_PAST:C_PAST + P].unsqueeze(1).to_broadcast([P, NH, P]), ALU.mult)
                        sp_.then_inc(sp_ready, 1)
                        dve.wait_ge(sp_ready, M + 1)
                        if m == 0 or m == i:
                            v.memset(pg[:, 0:1], 0.0).then_inc(acc_ready, 1)
                        else:
                            prev = spb[(M - 1) % 2] if m == 1 else accb[M % 2]
                            if M >= 1:
                                dve.wait_ge(sb_summed, M)
                            v.tensor_tensor(accb[(M + 1) % 2], prev, spb[M % 2], ALU.add).then_inc(acc_ready, 1)
                            dve.wait_ge(acc_ready, M + 1)
                        experts("sb", (t, m))
                    dve.wait_ge(pv_done, 12 * (T + 1))
                    dve.wait_ge(probs, 12 * (T + 1))
                    if T >= 1:
                        dve.wait_ge(o_turned, T)
                    dve.wait_ge(gates_ready, g + 1)
                    after(v.tensor_scalar(rden[:, :], den[:, T % 2, :], 1e-30, None, ALU.max))
                    after(v.reciprocal(rden[:, :], rden[:, :]))
                    after(v.tensor_tensor(rden[:, 0:12].rearrange("p (c h) -> p c h", c=3),
                                          rden[:, 0:12].rearrange("p (c h) -> p c h", c=3),
                                          gates[:, t, :].rearrange("p (h c) -> p c h", c=3), ALU.mult))
                    ob = bank(6 + T % 2)

                    def scaled(dst, col, c):
                        return v.tensor_tensor(dst.rearrange("p (h d) -> p h d", h=NH),
                                               ob[:, col:col + P].rearrange("p (h d) -> p h d", h=NH),
                                               rden[:, 4 * c:4 * c + 4].unsqueeze(2).to_broadcast([P, NH, HD]), ALU.mult)

                    tmp = zc[:, :, :].rearrange("p a b -> p (a b)")
                    o_nsa = o_row[:, P:2 * P]
                    scaled(o_nsa, 0, 0)
                    after(scaled(tmp[:, 0:P], 384, 1))
                    after(v.tensor_tensor(o_nsa, o_nsa, tmp[:, 0:P], ALU.add))
                    after(scaled(tmp[:, 0:P], 128, 2))
                    after(v.tensor_tensor(o_nsa, o_nsa, tmp[:, 0:P], ALU.add))
                    scaled(o_row[:, 2 * P:3 * P], 256, 3).then_inc(o_rows_v, 1)
                for sec, (sg, t0, nt) in enumerate(SECTIONS):
                    if sg == g:
                        section(sec)
            expert_gates(len(SECTIONS) - 1)
            expert_steps(len(SECTIONS) - 1, range(steps_of(len(SECTIONS) - 1)))


def kernel(**inputs):
    import numpy as np
    import concourse.bacc as bacc
    from concourse.bass_utils import run_bass_kernel_spmd as run

    a = {k: np.asarray(val) for k, val in inputs.items()}
    L = DEPTH

    def slices(w):
        n = w.shape[2]
        return np.ascontiguousarray(w.reshape(L, KC, P, n).transpose(0, 2, 1, 3)).reshape(L, P, KC * n)

    w = a["w_in"]
    col = lambda lo, hi: w[:, :, lo:hi]
    attn_a = slices(np.concatenate([col(0, 128), col(128, 256), col(384, 512), col(716, 844)], axis=2))
    attn_b = slices(np.concatenate([col(512, 544), col(544, 576), col(576, 608), col(640, 672), col(844, 876),
                                    col(256, 384), col(608, 640), col(672, 704), col(876, 908), col(704, 716)], axis=2))
    cmp_w = np.concatenate([slices(a["nsa_w_ck"]), slices(a["nsa_w_cv"]),
                            slices(a["nsa_pe_k"].reshape(L, D, 1)), slices(a["nsa_pe_v"].reshape(L, D, 1))], axis=2)
    merge = []
    for hf in range(2):
        for b, name in enumerate(("w_br_sb", "w_br_nsa", "w_br_moba")):
            lo = 908 + 1024 * b + 512 * hf
            merge.append(np.concatenate([slices(col(lo, lo + 512)), a[name][:, :, 512 * hf:512 * (hf + 1)]], axis=2))
    halves = lambda m: np.stack([slices(m[:, :, 0:512]), slices(m[:, :, 512:1024])], axis=1)
    kk = np.stack([a["peer_k1"], a["peer_k2"]], axis=2)
    arrays = {
        "consts": constants(),
        "x": a["x"].reshape(SEQ, D),
        "attn_a": attn_a,
        "attn_b": np.concatenate([attn_b, cmp_w], axis=2),
        "merge": np.stack(merge, axis=1),
        "w_out_h": halves(a["w_out"]),
        "ln1": np.concatenate([a["ln1_g"], a["ln1_b"]], axis=1).reshape(L, 2, D),
        "w_query": halves(a["peer_wq"].reshape(L, D, D)),
        "keys_T": np.ascontiguousarray(kk.transpose(0, 4, 1, 2, 3)).reshape(L, P, 8 * NKEYS),
        "table_u": a["peer_u"].reshape(L * N_EXPERTS, D),
        "table_v": a["peer_v"].reshape(L * N_EXPERTS, D),
        "ln2": np.concatenate([a["ln2_g"], a["ln2_b"]], axis=1).reshape(L, 2, D),
    }
    nc = bacc.Bacc("TRN2", target_bir_lowering=False, num_devices=1, dynamic_dma_scratch_size=8192)
    arrays = {k: np.ascontiguousarray(val) for k, val in arrays.items()}
    t = {k: nc.dram_tensor(f"in_{k}", val.shape, F32, kind="ExternalInput").ap() for k, val in arrays.items()}
    o = nc.dram_tensor("out_rows", (SEQ, D), F32, kind="ExternalOutput").ap()
    hybrid_layers(nc, t["consts"], t["x"], t["attn_a"], t["attn_b"], t["merge"], t["w_out_h"], t["ln1"],
                  t["w_query"], t["keys_T"], t["table_u"], t["table_v"], t["ln2"], o)
    r = run(nc, [{f"in_{k}": val for k, val in arrays.items()}], core_ids=[0])
    return r.results[0]["out_rows"].reshape(1, SEQ, D)
```
